# Optimizing a Trainium2 kernel written in Bass

```python
import jax, jax.numpy as jnp
from jax import lax
import numpy as np

D_MODEL = 1024
BATCH = 1
SEQ = 1024
DEPTH = 2

GRID_W = 64
CTX_LEN = 256
N_MIXERS = 4
EPS = 1e-6
ROPE_THETA = 10000.0
BLOCK = 128
N_FOURIER_GROUPS = 4
FOURIER_GROUP = D_MODEL // N_FOURIER_GROUPS
CONV_WIDTH = 3
MLA_HEADS = 16
MLA_Q_RANK = 256
MLA_KV_RANK = 128
MLA_NOPE = 128
MLA_ROPE = 64
MLA_V = 128
MLA_SCALE = (MLA_NOPE + MLA_ROPE) ** -0.5
GQA_Q_HEADS = 16
GQA_KV_HEADS = 4
GQA_GROUP = GQA_Q_HEADS // GQA_KV_HEADS
GQA_HEAD_DIM = 64
GQA_SCALE = GQA_HEAD_DIM ** -0.5
WINDOW = 128
N_EXPERTS = 16
N_EXPERT_GROUPS = 4
EXPERTS_PER_GROUP = N_EXPERTS // N_EXPERT_GROUPS
TOP_K = 2
EXPERT_FF = 256
N_FOURIER_LAYERS = (DEPTH + 3) // N_MIXERS
N_CONV_LAYERS = (DEPTH + 2) // N_MIXERS
N_MLA_LAYERS = (DEPTH + 1) // N_MIXERS
N_GQA_LAYERS = DEPTH // N_MIXERS

kernel_name = "hybrid_interleaved_diffusion_backbone"

def _rmsnorm(x, g):
    xf = x.astype(jnp.float32)
    y = xf * lax.rsqrt(jnp.mean(xf * xf, axis=-1, keepdims=True) + EPS)
    return (y * g.astype(jnp.float32)).astype(x.dtype)

def _axial_rope_tables(n_tokens, dim):
    rows = n_tokens // GRID_W
    row = jnp.repeat(jnp.arange(rows, dtype=jnp.float32), GRID_W)
    col = jnp.tile(jnp.arange(GRID_W, dtype=jnp.float32), rows)
    q = dim // 4
    inv = ROPE_THETA ** (-jnp.arange(q, dtype=jnp.float32) / q)
    ang = jnp.stack([row[:, None] * inv, col[:, None] * inv], axis=1)
    return jnp.cos(ang), jnp.sin(ang)

def _apply_axial_rope(x, cos, sin):
    q = x.shape[-1] // 4
    xr = x.reshape(*x.shape[:-1], 2, 2, q)
    x1, x2 = xr[..., 0, :], xr[..., 1, :]
    extra = (1,) * (x.ndim - 3)
    c = cos.reshape(cos.shape[0], *extra, 2, q).astype(x.dtype)
    s = sin.reshape(sin.shape[0], *extra, 2, q).astype(x.dtype)
    out = jnp.stack([x1 * c - x2 * s, x2 * c + x1 * s], axis=-2)
    return out.reshape(x.shape)

def _fourier_mix(h, w_out):
    b, l, d = h.shape
    hg = h.astype(jnp.float32).reshape(b, l, N_FOURIER_GROUPS, FOURIER_GROUP)
    f = jnp.fft.fft2(hg, axes=(1, 3), norm="ortho").real
    return f.reshape(b, l, d).astype(h.dtype) @ w_out

def _short_conv_mix(h, w_in, conv_w, w_out):
    b_gate, c_gate, xv = jnp.split(h @ w_in, 3, axis=-1)
    u = c_gate * xv
    up = jnp.pad(u, ((0, 0), (1, 1), (0, 0)))
    z = conv_w[0] * up[:, :-2] + conv_w[1] * up[:, 1:-1] + conv_w[2] * up[:, 2:]
    return (b_gate * z) @ w_out

def _mla_q(h, w_in, q_norm, w_uq, q_gain, cos, sin):
    b, l, _ = h.shape
    cq = _rmsnorm(h @ w_in[:, :MLA_Q_RANK], q_norm)
    q = (cq @ w_uq).reshape(b, l, MLA_HEADS, MLA_NOPE + MLA_ROPE)
    q_nope = _rmsnorm(q[..., :MLA_NOPE], q_gain[:MLA_NOPE])
    q_rope = _rmsnorm(q[..., MLA_NOPE:], q_gain[MLA_NOPE:])
    if cos is not None:
        q_rope = _apply_axial_rope(q_rope, cos, sin)
    return q_nope, q_rope

def _mla_kv(h, w_in, kv_norm, w_ukv, k_gain, cos, sin):
    b, l, _ = h.shape
    ckr = h @ w_in[:, MLA_Q_RANK:]
    ckv = _rmsnorm(ckr[..., :MLA_KV_RANK], kv_norm)
    kv = (ckv @ w_ukv).reshape(b, l, MLA_HEADS, MLA_NOPE + MLA_V)
    k_nope = _rmsnorm(kv[..., :MLA_NOPE], k_gain[:MLA_NOPE])
    v = kv[..., MLA_NOPE:]
    k_rope = _rmsnorm(ckr[..., MLA_KV_RANK:], k_gain[MLA_NOPE:])
    if cos is not None:
        k_rope = _apply_axial_rope(k_rope, cos, sin)
    return k_nope, k_rope, v

def _mla_softmax(qn, qr, kn, kr, v):
    s = (jnp.einsum('bqhd,bkhd->bhqk', qn, kn, preferred_element_type=jnp.float32)
         + jnp.einsum('bqhd,bkd->bhqk', qr, kr, preferred_element_type=jnp.float32)) * MLA_SCALE
    p = jax.nn.softmax(s, axis=-1).astype(v.dtype)
    return jnp.einsum('bhqk,bkhd->bqhd', p, v)

def _mla_latent_attention(q_nope, q_rope, k_nope, k_rope, v):
    b, l = q_nope.shape[:2]
    nb = l // BLOCK

    def blocks(t):
        return jnp.moveaxis(t.reshape(b, nb, BLOCK, *t.shape[2:]), 1, 0)

    out = lax.map(lambda a: _mla_softmax(a[0], a[1], k_nope, k_rope, v), (blocks(q_nope), blocks(q_rope)))
    return jnp.moveaxis(out, 0, 1).reshape(b, l, MLA_HEADS * MLA_V)

def _gqa_q(h, w_in, q_gain, cos, sin):
    b, l, _ = h.shape
    q = _rmsnorm((h @ w_in[:, :GQA_Q_HEADS * GQA_HEAD_DIM]).reshape(b, l, GQA_Q_HEADS, GQA_HEAD_DIM), q_gain)
    if cos is not None:
        q = _apply_axial_rope(q, cos, sin)
    return q

def _gqa_kv(h, w_in, k_gain, cos, sin):
    b, l, _ = h.shape
    kv = (h @ w_in[:, GQA_Q_HEADS * GQA_HEAD_DIM:]).reshape(b, l, 2, GQA_KV_HEADS, GQA_HEAD_DIM)
    k = _rmsnorm(kv[:, :, 0], k_gain)
    v = kv[:, :, 1]
    if cos is not None:
        k = _apply_axial_rope(k, cos, sin)
    return k, v

def _window_attention(q, k, v, kc, vc, sink):
    b, l = q.shape[:2]
    lc = kc.shape[1]
    nb = l // BLOCK
    qb = q.reshape(b, nb, BLOCK, GQA_KV_HEADS, GQA_GROUP, GQA_HEAD_DIM)

    def band(t):
        tp = jnp.pad(t, ((0, 0), (BLOCK, BLOCK), (0, 0), (0, 0))).reshape(b, nb + 2, BLOCK, GQA_KV_HEADS, GQA_HEAD_DIM)
        return jnp.concatenate([tp[:, :-2], tp[:, 1:-1], tp[:, 2:]], axis=2)

    kw, vw = band(k), band(v)
    qpos = jnp.arange(nb)[:, None] * BLOCK + jnp.arange(BLOCK)[None, :]
    kpos = jnp.arange(nb)[:, None] * BLOCK - BLOCK + jnp.arange(3 * BLOCK)[None, :]
    valid = ((jnp.abs(qpos[:, :, None] - kpos[:, None, :]) <= WINDOW)
             & (kpos[:, None, :] >= 0) & (kpos[:, None, :] < l))
    s_band = jnp.einsum('bnqhgd,bnkhd->bnhgqk', qb, kw, preferred_element_type=jnp.float32) * GQA_SCALE
    s_band = jnp.where(valid[None, :, None, None], s_band, -1e30)
    s_ctx = jnp.einsum('bnqhgd,bchd->bnhgqc', qb, kc, preferred_element_type=jnp.float32) * GQA_SCALE
    s_sink = jnp.broadcast_to(sink.astype(jnp.float32).reshape(GQA_KV_HEADS, GQA_GROUP)[None, None, :, :, None, None],
                              s_ctx.shape[:-1] + (1,))
    p = jax.nn.softmax(jnp.concatenate([s_ctx, s_band, s_sink], axis=-1), axis=-1).astype(v.dtype)
    out = (jnp.einsum('bnhgqc,bchd->bnqhgd', p[..., :lc], vc)
           + jnp.einsum('bnhgqk,bnkhd->bnqhgd', p[..., lc:lc + 3 * BLOCK], vw))
    return out.reshape(b, l, GQA_Q_HEADS * GQA_HEAD_DIM)

def _ctx_sink_attention(qc, kc, vc, sink):
    b, lc = qc.shape[:2]
    qg = qc.reshape(b, lc, GQA_KV_HEADS, GQA_GROUP, GQA_HEAD_DIM)
    s = jnp.einsum('bqhgd,bkhd->bhgqk', qg, kc, preferred_element_type=jnp.float32) * GQA_SCALE
    s_sink = jnp.broadcast_to(sink.astype(jnp.float32).reshape(GQA_KV_HEADS, GQA_GROUP)[None, :, :, None, None],
                              s.shape[:-1] + (1,))
    p = jax.nn.softmax(jnp.concatenate([s, s_sink], axis=-1), axis=-1)[..., :-1].astype(vc.dtype)
    return jnp.einsum('bhgqk,bkhd->bqhgd', p, vc).reshape(b, lc, GQA_Q_HEADS * GQA_HEAD_DIM)

def _moe(h, router_w, router_bias, w_gate, w_up, w_down):
    n = h.shape[0]
    scores = jax.nn.sigmoid((h @ router_w).astype(jnp.float32))
    biased = (scores + router_bias.astype(jnp.float32)).reshape(n, N_EXPERT_GROUPS, EXPERTS_PER_GROUP)
    group_score = lax.top_k(biased, TOP_K)[0].sum(-1)
    best = jnp.argmax(group_score, axis=-1)
    in_group = jax.nn.one_hot(best, N_EXPERT_GROUPS, dtype=jnp.float32)[:, :, None] > 0
    masked = jnp.where(in_group, biased, -jnp.inf).reshape(n, N_EXPERTS)
    _, idx = lax.top_k(masked, TOP_K)
    w = jnp.take_along_axis(scores, idx, axis=-1)
    w = w / jnp.sum(w, axis=-1, keepdims=True)
    comb = jnp.sum(jax.nn.one_hot(idx, N_EXPERTS, dtype=jnp.float32) * w[..., None], axis=1).astype(h.dtype)
    y = jnp.zeros_like(h)
    for e in range(N_EXPERTS):
        he = jax.nn.silu(h @ w_gate[e]) * (h @ w_up[e])
        y = y + comb[:, e:e + 1] * (he @ w_down[e])
    return y

def setup_inputs(seed: int = 0) -> dict:
    key = jax.random.key(seed)
    ks = jax.random.split(key, 32)
    f32 = jnp.float32
    D = D_MODEL

    def w(k, shape, fan_in, gain=1.0):
        return jax.random.normal(k, shape, f32) * (gain * fan_in ** -0.5)

    def g(k, shape):
        return 1.0 + 0.02 * jax.random.normal(k, shape, f32)

    gqa_in = (GQA_Q_HEADS + 2 * GQA_KV_HEADS) * GQA_HEAD_DIM
    return {
        "x": jax.random.normal(ks[0], (BATCH, SEQ, D), f32),
        "c": jax.random.normal(ks[1], (BATCH, D), f32),
        "ctx": jax.random.normal(ks[2], (BATCH, CTX_LEN, D), f32),
        "c_ctx": jax.random.normal(ks[3], (D,), f32),
        "w_ada": w(ks[4], (DEPTH, D, 6 * D), D, 0.5),
        "b_ada": 0.02 * jax.random.normal(ks[5], (DEPTH, 6 * D), f32),
        "norm_mix": g(ks[6], (DEPTH, D)),
        "norm_ffn": g(ks[7], (DEPTH, D)),
        "fourier_w_out": w(ks[8], (N_FOURIER_LAYERS, D, D), D),
        "conv_w_in": w(ks[9], (N_CONV_LAYERS, D, 3 * D), D),
        "conv_w": w(ks[10], (N_CONV_LAYERS, CONV_WIDTH, D), CONV_WIDTH),
        "conv_w_out": w(ks[11], (N_CONV_LAYERS, D, D), D),
        "mla_w_in": w(ks[12], (N_MLA_LAYERS, D, MLA_Q_RANK + MLA_KV_RANK + MLA_ROPE), D),
        "mla_q_norm": g(ks[13], (N_MLA_LAYERS, MLA_Q_RANK)),
        "mla_kv_norm": g(ks[14], (N_MLA_LAYERS, MLA_KV_RANK)),
        "mla_w_uq": w(ks[15], (N_MLA_LAYERS, MLA_Q_RANK, MLA_HEADS * (MLA_NOPE + MLA_ROPE)), MLA_Q_RANK),
        "mla_w_ukv": w(ks[16], (N_MLA_LAYERS, MLA_KV_RANK, MLA_HEADS * (MLA_NOPE + MLA_V)), MLA_KV_RANK),
        "mla_q_gain": g(ks[17], (N_MLA_LAYERS, MLA_NOPE + MLA_ROPE)),
        "mla_k_gain": g(ks[18], (N_MLA_LAYERS, MLA_NOPE + MLA_ROPE)),
        "mla_w_out": w(ks[19], (N_MLA_LAYERS, MLA_HEADS * MLA_V, D), MLA_HEADS * MLA_V),
        "gqa_w_in": w(ks[20], (N_GQA_LAYERS, D, gqa_in), D),
        "gqa_q_gain": g(ks[21], (N_GQA_LAYERS, GQA_HEAD_DIM)),
        "gqa_k_gain": g(ks[22], (N_GQA_LAYERS, GQA_HEAD_DIM)),
        "gqa_sink": 0.5 * jax.random.normal(ks[23], (N_GQA_LAYERS, GQA_Q_HEADS), f32),
        "gqa_w_out": w(ks[24], (N_GQA_LAYERS, GQA_Q_HEADS * GQA_HEAD_DIM, D), GQA_Q_HEADS * GQA_HEAD_DIM),
        "router_w": w(ks[25], (D, N_EXPERTS), D),
        "router_bias": 0.01 * jax.random.normal(ks[26], (N_EXPERTS,), f32),
        "moe_w_gate": w(ks[27], (DEPTH, N_EXPERTS, D, EXPERT_FF), D),
        "moe_w_up": w(ks[28], (DEPTH, N_EXPERTS, D, EXPERT_FF), D),
        "moe_w_down": w(ks[29], (DEPTH, N_EXPERTS, EXPERT_FF, D), EXPERT_FF),
    }

def reference(x, c, ctx, c_ctx, w_ada, b_ada, norm_mix, norm_ffn, fourier_w_out, conv_w_in, conv_w, conv_w_out,
              mla_w_in, mla_q_norm, mla_kv_norm, mla_w_uq, mla_w_ukv, mla_q_gain, mla_k_gain, mla_w_out,
              gqa_w_in, gqa_q_gain, gqa_k_gain, gqa_sink, gqa_w_out, router_w, router_bias,
              moe_w_gate, moe_w_up, moe_w_down):
    b, l, d = x.shape
    lc = ctx.shape[1]
    cos_m, sin_m = _axial_rope_tables(l, MLA_ROPE)
    cos_g, sin_g = _axial_rope_tables(l, GQA_HEAD_DIM)
    silu_c = jax.nn.silu(c)
    silu_cc = jax.nn.silu(c_ctx)
    for i in range(DEPTH):
        kind, j = i % N_MIXERS, i // N_MIXERS
        ctx_next = i < DEPTH - 1
        need_hc = ctx_next or kind >= 2
        sh1, sc1, g1, sh2, sc2, g2 = jnp.split((silu_c @ w_ada[i] + b_ada[i])[:, None, :], 6, axis=-1)
        hx = _rmsnorm(x, norm_mix[i]) * (1 + sc1) + sh1
        if need_hc:
            csh1, csc1, cg1, csh2, csc2, cg2 = jnp.split(silu_cc @ w_ada[i] + b_ada[i], 6, axis=-1)
            hc = _rmsnorm(ctx, norm_mix[i]) * (1 + csc1) + csh1
        if kind == 0:
            yx = _fourier_mix(hx, fourier_w_out[j])
            if ctx_next:
                yc = _fourier_mix(hc, fourier_w_out[j])
        elif kind == 1:
            yx = _short_conv_mix(hx, conv_w_in[j], conv_w[j], conv_w_out[j])
            if ctx_next:
                yc = _short_conv_mix(hc, conv_w_in[j], conv_w[j], conv_w_out[j])
        elif kind == 2:
            kn_c, kr_c, v_c = _mla_kv(hc, mla_w_in[j], mla_kv_norm[j], mla_w_ukv[j], mla_k_gain[j], None, None)
            kn_x, kr_x, v_x = _mla_kv(hx, mla_w_in[j], mla_kv_norm[j], mla_w_ukv[j], mla_k_gain[j], cos_m, sin_m)
            qn_x, qr_x = _mla_q(hx, mla_w_in[j], mla_q_norm[j], mla_w_uq[j], mla_q_gain[j], cos_m, sin_m)
            kn = jnp.concatenate([kn_c, kn_x], axis=1)
            kr = jnp.concatenate([kr_c, kr_x], axis=1)
            vv = jnp.concatenate([v_c, v_x], axis=1)
            yx = _mla_latent_attention(qn_x, qr_x, kn, kr, vv) @ mla_w_out[j]
            if ctx_next:
                qn_c, qr_c = _mla_q(hc, mla_w_in[j], mla_q_norm[j], mla_w_uq[j], mla_q_gain[j], None, None)
                yc = _mla_softmax(qn_c, qr_c, kn_c, kr_c, v_c).reshape(b, lc, MLA_HEADS * MLA_V) @ mla_w_out[j]
        else:
            kc, vc = _gqa_kv(hc, gqa_w_in[j], gqa_k_gain[j], None, None)
            kx, vx = _gqa_kv(hx, gqa_w_in[j], gqa_k_gain[j], cos_g, sin_g)
            qx = _gqa_q(hx, gqa_w_in[j], gqa_q_gain[j], cos_g, sin_g)
            yx = _window_attention(qx, kx, vx, kc, vc, gqa_sink[j]) @ gqa_w_out[j]
            if ctx_next:
                qc = _gqa_q(hc, gqa_w_in[j], gqa_q_gain[j], None, None)
                yc = _ctx_sink_attention(qc, kc, vc, gqa_sink[j]) @ gqa_w_out[j]
        x = x + g1 * yx
        hx = _rmsnorm(x, norm_ffn[i]) * (1 + sc2) + sh2
        if ctx_next:
            ctx = ctx + cg1 * yc
            hc = _rmsnorm(ctx, norm_ffn[i]) * (1 + csc2) + csh2
            tokens = jnp.concatenate([hc.reshape(-1, d), hx.reshape(-1, d)], axis=0)
            y = _moe(tokens, router_w, router_bias, moe_w_gate[i], moe_w_up[i], moe_w_down[i])
            ctx = ctx + cg2 * y[:b * lc].reshape(b, lc, d)
            x = x + g2 * y[b * lc:].reshape(b, l, d)
        else:
            y = _moe(hx.reshape(-1, d), router_w, router_bias, moe_w_gate[i], moe_w_up[i], moe_w_down[i])
            x = x + g2 * y.reshape(b, l, d)
    return x


_drawn_inputs = setup_inputs


def setup_inputs(seed=0):
    import zlib

    import numpy as np

    out = dict(_drawn_inputs(seed))
    spreads = {}
    factors = {}
    for name, (base, spread) in spreads.items():
        noise = np.random.default_rng([zlib.crc32(name.encode()), seed]).standard_normal(out[name].shape)
        drawn = base * np.exp(spread * noise) if base else spread * noise
        out[name] = __import__('jax').numpy.asarray(drawn.astype(out[name].dtype))
    for name, factor in factors.items():
        out[name] = (out[name] * factor).astype(out[name].dtype)
    return out
```

```python
import numpy as np
from contextlib import ExitStack

import concourse.bass as bass
from concourse import mybir

P = 128
SEQ, D = 1024, 1024
NT = SEQ // P
NC = D // P
BANK = 512
GROUPS, GROUP = 4, 256
EXPERTS, EGROUPS, PER_GROUP, TOP = 16, 4, 4, 2
FF = 256
PAIRS = SEQ * TOP
MAX_SLOTS = (PAIRS + EXPERTS * (P - 1)) // P
ADA = 6 * D
ADA_BLOCK = 256
N_ADA = ADA // ADA_BLOCK
EPS = 1e-6
TILES = [(1, 2), (257, 2), (513, 2), (769, 2), (2, 4), (514, 4), (4, 8), (0, 8)]
N_FOLD = 384
N_FREQ = 640
N_TABLE = 4 * 512 + 2 * 256 + 256 + 256 + 6 * P


def dft_tables():
    n = np.arange(512)[:, None]

    def pos(rows, k):
        a = 2 * np.pi * ((n[:rows] * k[None, :]) % SEQ) / SEQ
        t = np.concatenate([np.cos(a), np.sin(a)], 1) / np.sqrt(SEQ * GROUP)
        return t.reshape(rows // P, P, -1).transpose(1, 0, 2).reshape(P, -1)

    j = np.arange(256)
    parts = [pos(512, 2 * j + 1), pos(256, 4 * j[:128] + 2), pos(128, 8 * j[:128] + 4), pos(128, 8 * j[:128])]
    d = np.arange(P)[:, None]
    for parity in range(2):
        a = 2 * np.pi * ((d * (2 * j[None, :128] + parity)) % GROUP) / GROUP
        parts += [np.cos(a), np.sin(a), -np.sin(a)]
    return np.concatenate(parts, 1).astype(np.float32)


C_IDENT, C_ONES, C_LOWER, C_ROW = 0, 128, 256, 384
C_PRIO, C_TRI, C_STEP, C_TOKEN, C_SLOT = 512, 516, 772, 780, 788
N_CONST = 788 + 40


def shape_constants():
    t = np.zeros((P, N_CONST), np.float32)
    i = np.arange(P)
    t[:, C_IDENT:C_IDENT + P] = np.eye(P)
    t[:, C_ONES:C_ONES + P] = 1
    t[:, C_LOWER:C_LOWER + P] = i[:, None] < i[None, :]
    t[:, C_ROW:C_ROW + P] = i
    t[:, C_PRIO:C_PRIO + PER_GROUP] = PER_GROUP - np.arange(PER_GROUP)
    e = np.arange(EXPERTS)
    t[:, C_TRI:C_TRI + EXPERTS ** 2] = (e[None, :] < e[:, None]).reshape(-1)
    t[:, C_STEP:C_STEP + NT] = P * np.arange(NT)
    t[:, C_TOKEN:C_TOKEN + NT] = i[:, None] + P * np.arange(NT)
    t[:, C_SLOT:C_SLOT + 40] = np.arange(40)
    return t


def backbone(nc, x, c, w_ada, b_ada, norm_mix, norm_ffn, fourier_w_out, conv_w_in, conv_w, conv_w_out,
             router_w, router_bias, moe_w_gate, moe_w_up, moe_w_down, tables, constants, out):
    f32, i32, u32 = mybir.dt.float32, mybir.dt.int32, mybir.dt.uint32
    ALU, ACT, X_AXIS = mybir.AluOpType, mybir.ActivationFunctionType, mybir.AxisListType.X
    top = ExitStack()
    ds = bass.ds

    def sem(name):
        return top.enter_context(nc.semaphore(name))

    def width(shape):
        n = 4
        for k in shape[1:]:
            n *= k
        return n

    class Region:

        def __init__(self, start):
            self.at = start

        def put(self, name, shape, dt=f32):
            t = nc.alloc_sbuf_tensor_at(name, shape, dt, offset=self.at)
            self.at += (width(shape) + 31) // 32 * 32
            return t

    x_rows, out_rows = x[0], out[0]

    arena = top.enter_context(nc.sbuf_tensor("arena", [P, (nc.sbuf_bytes_remaining - 1024) // 4], f32))
    base = (nc.sbuf_base - width(arena.shape) + 31) // 32 * 32
    keep = Region(base)
    X = keep.put("X", [P, NT, D])
    XS = [keep.put(f"XS{i}", [P, D]) for i in range(2)]
    ROWS = keep.put("ROWS", [P, 4, D])
    G1, GS2, SH2, G2 = (ROWS[:, i, :] for i in range(4))
    K = keep.put("K", [P, N_CONST])
    ident, ones, lower = (K[:, a:a + P] for a in (C_IDENT, C_ONES, C_LOWER))
    RW = keep.put("RW", [P, NC, EXPERTS])
    RB = keep.put("RB", [P, EXPERTS])
    CW = keep.put("CW", [P, 3, NC])
    CC = keep.put("CC", [P, NC])
    SC = keep.put("SC", [P, NC])
    NM = keep.put("NM", [P, 2, NC])
    BC = keep.put("BC", [P, 2 * NC])
    AC = keep.put("AC", [P, 2, NC])
    SS, VAR, SD, RS, RT = (keep.put(n, [P, NT]) for n in ("SS", "VAR", "SD", "RS", "RT"))
    TOKI = keep.put("TOKI", [P, MAX_SLOTS], u32)
    WOF = keep.put("WOF", [P, MAX_SLOTS])
    SEID = keep.put("SEID", [P, MAX_SLOTS + 1], i32)
    POSI = keep.put("POSI", [P, TOP, NT], u32)
    SQ = keep.put("SQ", [P, D])
    ada_at = keep.at
    ACC = keep.put("ACC", [P, ADA])
    WA = [keep.put(f"WA{i}", [P, NC, ADA_BLOCK]) for i in range(2)]
    fourier_at = keep.at
    NF = keep.put("NF", [P, D])
    phase = keep.at

    PT = Region(base).put("PT", [P, NC, 2, N_FREQ])
    r = Region(base + width(PT.shape))
    FAB = r.put("FAB", [P, 2, D])
    FAA = r.put("FAA", [P, 2, D])
    r = Region(fourier_at)
    XN = r.put("XN", [P, NT, D])
    fold_at = r.at
    FB = r.put("FB", [P, 4, D])
    fa_at = r.at
    FA = r.put("FA", [P, 4, D])
    TB = r.put("TB", [P, N_TABLE])
    EF = [r.put(f"EF{i}", [P, 2, 2, N_FREQ]) for i in range(2)]
    assert r.at <= base + width(arena.shape) - 32, (r.at - base, width(arena.shape))
    r = Region(fa_at)
    FAAB = r.put("FAAB", [P, D])
    FAAA = r.put("FAAA", [P, D])
    FT = Region(fourier_at).put("FT", [P, NC, SEQ])
    WF = Region(fold_at).put("WF", [P, NC, D])
    VS = Region(ada_at - width(SQ.shape)).put("VS", [P, 2, N_FOLD])

    r = Region(phase)
    WGU = [r.put(f"WGU{i}", [P, NC, 2 * FF]) for i in range(2)]
    WD = [r.put(f"WD{i}", [P, FF // P, D]) for i in range(2)]
    slots_at = r.at
    XG = [r.put(f"XG{i}", [P, D]) for i in range(2)]
    XT = [r.put(f"XT{i}", [P, NC, P]) for i in range(2)]
    YO = [r.put(f"YO{i}", [P, D]) for i in range(2)]
    HE = [r.put(f"HE{i}", [P, FF]) for i in range(2)]
    HET = [r.put(f"HET{i}", [P, FF // P, P]) for i in range(2)]
    SG = r.put("SG", [P, FF])
    r = Region(slots_at)
    H = [r.put(f"H{i}", [P, D]) for i in range(4)]
    HTM = [r.put(f"HTM{i}", [P, NC, P]) for i in range(2)]
    ROWHOT = r.put("ROWHOT", [P, TOP * NT, P])
    SLOTHOT = r.put("SLOTHOT", [P, TOP * NT, 2, MAX_SLOTS])
    r = Region(phase)
    SMALL = r.put("SMALL", [P, 24, NT, EXPERTS])
    TINY = r.put("TINY", [P, 24, 40])
    assert r.at <= base + width(arena.shape) - 32, (r.at - base, width(arena.shape))
    CG = [Region(phase + 4096 * i).put(f"CG{i}", [P, D]) for i in range(4)]

    r = Region(phase)
    HT = r.put("HT", [P, NC, SEQ])
    zt_at = r.at
    ZT = r.put("ZT", [P, NC, SEQ])
    WIN = [r.put(f"WIN{i}", [P, NC, 3, P]) for i in range(2)]
    CB = [r.put(f"CB{i}", [P, BANK]) for i in range(2)]
    U = r.put("U", [P, SEQ + 2])
    Z = Region(base + width(X.shape)).put("Z", [P, SEQ])
    assert r.at <= base + width(arena.shape) - 32, (r.at - base, width(arena.shape))
    BB = Region(base + width(X.shape) + width(Z.shape)).put("BB", [P, SEQ])
    XN2 = Region(zt_at).put("XN2", [P, NT, D])
    WOUT = Region(phase).put("WOUT", [P, NC, D])

    PS = top.enter_context(nc.psum_tensor("PS", [P, 8, BANK], f32))

    def bank(i, n=1):
        return PS[:, i:i + n, :].rearrange("p b n -> p (b n)")

    h_dram = [nc.dram_tensor(f"h_dram{i}", [SEQ, D], f32, kind="Internal").ap() for i in range(2)]
    y_dram = [nc.dram_tensor(f"y_dram{i}", [MAX_SLOTS * P, D], f32, kind="Internal").ap() for i in range(2)]

    consts_in, small_in, c_in, tables_in = sem("consts_in"), sem("small_in"), sem("c_in"), sem("tables_in")
    bias_in, norm_row_in, wf_in, out_done = (
        sem(n) for n in ("bias_in", "norm_row_in", "wf_in", "out_done"))
    wout_in = [sem(f"wout_in{i}") for i in range(4)]
    x_in = [sem(f"x_in{i}") for i in range(4)]
    res_in = [sem(f"res_in{i}") for i in range(NT)]
    wa_in = [sem(f"wa_in{i}") for i in range(2)]
    win_in = [sem(f"win_in{i}") for i in range(2)]
    h_stored = [sem(f"h_stored{i}") for i in range(4)]
    gathered = [[sem(f"gathered{layer}_{i}") for i in range(2)] for layer in range(2)]
    wgu_in = [sem(f"wgu_in{i}") for i in range(2)]
    wd_in = [sem(f"wd_in{i}") for i in range(2)]
    y_stored = [sem(f"y_stored{i}") for i in range(2)]
    cg_in = [sem(f"cg_in{i}") for i in range(4)]
    (acc_clear, wa_used, silu_c, sq_done, var_ready, sd_ready, folds, cols_mm, cols_ready, step1_mm, pt_act,
     pt_dve, ef_ready, step2_mm, vs_ready, ft_act, ft_dve, rows_mm, row_evac, y_mm, x_ready, h_ready, h_tr,
     hT_ready, router_mm, logits_sig, mask_ready, rank_mm, hot_ready, table_mm, routed, xt_tr, xt_act, xt_dve,
     gu_mm, silu_g, he_ready, he_tr, heT_ready, yd_mm, yo_ready, added, xn2_ready, conv_tr, hT_act,
     hT_dve, cin_mm, cb_ready, bb_ready, u_ready, z_ready, u_zero) = (
        sem(n) for n in ("acc_clear wa_used silu_c sq_done var_ready sd_ready folds cols_mm cols_ready step1_mm "
                         "pt_act pt_dve ef_ready step2_mm vs_ready ft_act ft_dve rows_mm row_evac y_mm x_ready "
                         "h_ready h_tr hT_ready router_mm logits_sig mask_ready rank_mm hot_ready table_mm routed "
                         "xt_tr xt_act xt_dve gu_mm silu_g he_ready he_tr heT_ready yd_mm yo_ready added "
                         "xn2_ready conv_tr hT_act hT_dve cin_mm cb_ready bb_ready u_ready z_ready u_zero").split())
    act_step, dve_step = sem("act_step"), sem("dve_step")

    block = top.enter_context(nc.Block())
    PAIR_LOOPS = (MAX_SLOTS - 3) // 2
    ADA_PAIRS = N_ADA // 2
    ADA_MIXER = 2 * D // ADA_BLOCK
    ALWAYS = PAIRS // P // 2
    SLOTS_OF = [(MAX_SLOTS + 1) // 2, MAX_SLOTS // 2]

    def load_ada(sp, layer, b, half, par):
        src = w_ada[layer].rearrange("(p k) n -> p k n", k=NC)[:, :, ds(b * ADA_BLOCK, ADA_BLOCK)]
        sp.dma_start(WA[par][:], src).then_inc(wa_in[par], 16)

    def slots_used(engine):
        return engine.value_load(SEID[0:1, MAX_SLOTS:MAX_SLOTS + 1], min_val=PAIRS // P, max_val=MAX_SLOTS)

    @block.sync
    def _(sp):
        sp.dma_start(K[:], constants).then_inc(consts_in, 16)
        xv = x_rows.rearrange("(t p) d -> p t d", p=P)
        for q in range(4):
            sp.dma_start(XN[:, q, :], xv[:, q, :]).then_inc(x_in[q], 16)
            sp.dma_start(XN[:, q + 4, :], xv[:, q + 4, :]).then_inc(x_in[q], 16)
        sp.dma_start(TB[:], tables).then_inc(tables_in, 16)
        for par in range(2):
            load_ada(sp, 0, par, 0, par)
        with sp.Fori(1, ADA_PAIRS) as i:
            for par in range(2):
                sp.wait_ge(wa_used, 2 * i + par - 1)
                load_ada(sp, 0, 2 * i + par, i, par)

        def expert_of(s):
            return sp.value_load(SEID[0:1, ds(s, 1)], min_val=0, max_val=EXPERTS - 1)

        def load_gate_up(layer, e, par):
            for j, w in enumerate((moe_w_gate, moe_w_up)):
                src = w[layer].rearrange("e d f -> (e d) f")[ds(e * D, D), :].rearrange("(c p) f -> p c f", p=P)
                sp.dma_start(WGU[par][:, :, j * FF:(j + 1) * FF], src).then_inc(wgu_in[par], 16)

        def load_down(layer, e, par):
            src = moe_w_down[layer].rearrange("e f d -> (e f) d")[ds(e * FF, FF), :].rearrange("(f p) d -> p f d", p=P)
            sp.dma_start(WD[par][:], src).then_inc(wd_in[par], 16)

        def store_y(layer, s, par):
            sp.dma_start(y_dram[layer][ds(s * P, P), :], YO[par][:]).then_inc(y_stored[par], 16)

        def slot(layer, s, par, first=False, load2=True, load1=True):
            b = layer * MAX_SLOTS
            e2 = expert_of(s + 2) if load2 else None
            e1 = expert_of(s + 1) if load1 else None
            if load2:
                sp.wait_ge(gu_mm, s + (b + 1))
                load_gate_up(layer, e2, par)
            if load1:
                if not first:
                    sp.wait_ge(yd_mm, s + b)
                load_down(layer, e1, 1 - par)
            if not first:
                sp.wait_ge(yo_ready, s + b)
                store_y(layer, s - 1, 1 - par)

        for layer in range(2):
            for m in range(NT):
                sp.wait_ge(h_ready, layer * NT + m + 1)
                sp.dma_start(h_dram[layer][m * P:(m + 1) * P, :], H[m % 4][:]).then_inc(h_stored[m % 4], 16)
            sp.wait_ge(routed, layer + 1)
            used = slots_used(sp)
            load_gate_up(layer, expert_of(0), 0)
            load_gate_up(layer, expert_of(1), 1)
            load_down(layer, expert_of(0), 0)
            slot(layer, 0, 0, first=True)

            def pair(i):
                for k in range(2):
                    slot(layer, 2 * i + (1 + k), 1 - k)

            def skip_pair(i):
                sp.wait_ge(yo_ready, 2 * i + layer * MAX_SLOTS)
                for par in range(2):
                    n = layer * SLOTS_OF[par]
                    sp.wait_ge(wgu_in[par], i * 32 + (2 - par + n) * 32)
                    sp.sem_inc(wgu_in[par], 32)
                    sp.wait_ge(wd_in[par], i * 16 + (1 + n) * 16)
                    sp.sem_inc(wd_in[par], 16)
                    sp.wait_ge(y_stored[par], i * 16 + n * 16)
                    store_y(layer, 2 * i + par, par)

            def pair_if_used(i):
                with sp.If(used > 2 * i):
                    pair(i)
                with sp.Else():
                    skip_pair(i)

            if layer == 0:
                with sp.Fori(0, ADA_MIXER // 2) as i:
                    for k in range(2):
                        slot(layer, 2 * i + (1 + k), 1 - k)
                        sp.wait_ge(wa_used, 2 * i + (N_ADA + k - 1))
                        load_ada(sp, 1, 2 * i + k, i, k)
            with sp.Fori(0 if layer else ADA_MIXER // 2, ALWAYS) as i:
                pair(i)
            with sp.Fori(ALWAYS, PAIR_LOOPS) as i:
                pair_if_used(i)
            with sp.If(used > 2 * PAIR_LOOPS):
                slot(layer, MAX_SLOTS - 2, 1, load2=False)
                slot(layer, MAX_SLOTS - 1, 0, load2=False, load1=False)
                slot(layer, MAX_SLOTS, 1, load2=False, load1=False)
            with sp.Else():
                sp.wait_ge(wd_in[0], (PAIR_LOOPS + 1 + layer * SLOTS_OF[0]) * 16)
                sp.sem_inc(wd_in[0], 16)
                sp.wait_ge(yo_ready, 2 * PAIR_LOOPS + layer * MAX_SLOTS)
                for s in range(2 * PAIR_LOOPS, MAX_SLOTS):
                    sp.wait_ge(y_stored[s % 2], (s // 2 + layer * SLOTS_OF[s % 2]) * 16)
                    store_y(layer, s, s % 2)
            if layer == 0:
                def load_win(j, par):
                    src = conv_w_in[0].rearrange("(c p) (s n) -> p c s n", p=P, s=3)
                    for s in range(3):
                        sp.dma_start(WIN[par][:, :, s, :], src[:, :, s, ds(j * P, P)]).then_inc(win_in[par], 16)

                def load_ada_pair(j):
                    for k in range(2):
                        sp.wait_ge(wa_used, 2 * j + (N_ADA + ADA_MIXER + k - 1))
                        load_ada(sp, 1, 2 * j + (ADA_MIXER + k), None, k)

                load_ada_pair(0)
                sp.wait_ge(added, 2 * NT)
                load_win(0, 0)
                load_win(1, 1)
                with sp.Fori(1, NC // 2) as i:
                    for k in range(2):
                        sp.wait_ge(cin_mm, 4 * i + (2 * k - 2))
                        load_win(2 * i + k, k)
                        load_ada_pair(2 * i + (k - 1))
                load_ada_pair(NC - 1)
                sp.wait_ge(cin_mm, 2 * NC)
                for q in range(4):
                    sp.dma_start(WOUT[:, 2 * q:2 * q + 2, :],
                                 conv_w_out[0, 2 * q * P:2 * (q + 1) * P, :].rearrange("(j p) n -> p j n", p=P)
                                 ).then_inc(wout_in[q], 16)
        for m, (first, step) in enumerate(TILES):
            sp.wait_ge(added, 2 * NT + 2 * (m + 1))
            sp.dma_start(out_rows[ds(first, P, step=step), :], X[:, m, :]).then_inc(out_done, 16)
        sp.wait_ge(out_done, 16 * NT)

    @block.gpsimd
    def _(pool):
        def bias_row(layer):
            pool.memset(ACC[:], 0.0).then_inc(acc_clear, 1)
            pool.wait_ge(acc_clear, layer + 1)
            pool.dma_start(ACC[0:1, :], b_ada[layer:layer + 1, :]).then_inc(bias_in, 16)

        bias_row(0)

        def gather(layer, s, par):
            pool.indirect_dma_start(out=XG[par][:], out_offset=None, in_=h_dram[layer],
                                    in_offset=bass.IndirectOffsetOnAxis(ap=TOKI[:, s:s + 1], axis=0)
                                    ).then_inc(gathered[layer][par], 16)

        def slot(layer, s, par):
            pool.wait_ge(xt_tr, s + (layer * MAX_SLOTS + 1))
            gather(layer, s + 2, par)

        for layer in range(2):
            if layer == 0:
                pool.wait_ge(rows_mm, 4)
                bias_row(1)
            for i in range(4):
                pool.wait_ge(h_stored[i], 32 * (layer + 1))
            pool.wait_ge(routed, layer + 1)
            used = slots_used(pool)
            gather(layer, 0, 0)
            gather(layer, 1, 1)
            for i in range(PAIR_LOOPS + 1):
                slots = range(2 * i, min(2 * i + 2, MAX_SLOTS - 2))
                if i < ALWAYS:
                    for s in slots:
                        slot(layer, s, s % 2)
                    continue
                with pool.If(used > 2 * i):
                    for s in slots:
                        slot(layer, s, s % 2)
            for par in range(2):
                pool.wait_ge(y_stored[par], 16 * SLOTS_OF[par] * (layer + 1))
            for q in range(TOP * NT):
                n = layer * TOP * NT + q
                if q >= 4:
                    pool.wait_ge(added, n - 3)
                pool.indirect_dma_start(out=CG[q % 4][:], out_offset=None, in_=y_dram[layer],
                                        in_offset=bass.IndirectOffsetOnAxis(ap=POSI[:, q % 2, q // 2:q // 2 + 1], axis=0)
                                        ).then_inc(cg_in[q % 4], 16)

    @block.scalar
    def _(act):
        count = [0]

        def link(ins):
            count[0] += 1
            ins.then_inc(act_step, 1)
            act.wait_ge(act_step, count[0])

        with nc.allow_non_contiguous_dma(reason="vectors by channel, a few KB"):
            act.dma_start(CC[:], c[0].rearrange("(p k) -> p k", k=NC)).then_inc(c_in, 16)
            for i in range(2):
                act.dma_start(NM[:, i, :], norm_mix[i].rearrange("(k p) -> p k", p=P)).then_inc(small_in, 16)
            act.dma_start(BC[:], b_ada[0, 0:2 * D].rearrange("(k p) -> p k", p=P)).then_inc(small_in, 16)
            act.dma_start(RW[:], router_w.rearrange("(k p) e -> p k e", p=P)).then_inc(small_in, 16)
            act.dma_start(RB[:], router_bias.partition_broadcast(P)).then_inc(small_in, 16)
            for t in range(3):
                act.dma_start(CW[:, t, :], conv_w[0, t].rearrange("(k p) -> p k", p=P)).then_inc(small_in, 16)
        act.wait_ge(c_in, 16)
        nc.scalar.activation(SC[:], CC[:], ACT.Silu).then_inc(silu_c, 1)

        def squares(src, m, done):
            count[0] += 1
            nc.scalar.activation(SQ[:], src, ACT.Square, accum_out=SS[:, m:m + 1]).then_inc(sq_done, 1)
            act.wait_ge(sq_done, done)

        def root(n):
            act.wait_ge(var_ready, n + 1)
            nc.scalar.activation(SD[:], VAR[:], ACT.Sqrt).then_inc(sd_ready, 1)

        for q in range(4):
            act.wait_ge(x_in[q], 32)
            squares(XN[:, q, :], q, 2 * q + 1)
            squares(XN[:, q + 4, :], q + 4, 2 * q + 2)
        root(0)

        def pt_evac(dt):
            b = 3 * (dt % 2)
            act.wait_ge(step1_mm, dt + 1)
            nc.scalar.activation(PT[:, dt, :, 0:256], bank(b).rearrange("p (s n) -> p s n", s=2), ACT.Copy,
                                 scale=AC[:, 1, dt:dt + 1]).then_inc(pt_act, 1)

        def mix_evac(ch):
            act.wait_ge(step2_mm, ch + 1)
            if ch >= 2:
                act.wait_ge(ft_dve, ch - 1)
            nc.scalar.activation(VS[:, ch % 2, :], bank(7)[:, 0:N_FOLD], ACT.Copy).then_inc(vs_ready, 1)
            nc.scalar.activation(FT[:, ch, 768:1024].rearrange("p (b n) -> p b n", b=2), PS[:, 6:8, N_FOLD:BANK],
                                 ACT.Copy).then_inc(ft_act, 1)

        act.wait_ge(cols_ready, 1)
        for dts, chs in (((0, 1, 2, 3), (0, 1)), ((4, 5), (2, 3)), ((6, 7), (4, 5, 6, 7))):
            for dt in dts:
                pt_evac(dt)
            if dts[-1] == 7:
                for g in range(GROUPS):
                    act.dma_start(WF[:, 2 * g:2 * g + 2, :],
                                  fourier_w_out[0, g * GROUP:(g + 1) * GROUP, :].rearrange("(j r) n -> j r n", r=2)
                                  ).then_inc(wf_in, 16)
                act.wait_ge(ef_ready, GROUPS)
                for m, (first, step) in enumerate(TILES):
                    act.dma_start(X[:, m, :], x_rows[ds(first, P, step=step), :]).then_inc(res_in[m], 16)
            for ch in chs:
                mix_evac(ch)

        def row_evac_act(n, row, b):
            act.wait_ge(rows_mm, n)
            nc.scalar.activation(row, bank(b, 2), ACT.Copy).then_inc(row_evac, 1)

        row_evac_act(1, G1, 6)

        for layer in range(2):
            for m in range(NT):
                act.wait_ge(x_ready, layer * NT + m + 1)
                squares(X[:, m, :], m, NT * (1 + 2 * layer) + m + 1)
            root(1 + 2 * layer)
            if layer == 0:
                act.dma_start(NF[:], norm_ffn[0].partition_broadcast(P)).then_inc(norm_row_in, 16)
                row_evac_act(2, SH2, 4)
                act.wait_ge(row_evac, 3)
                row_evac_act(4, G2, 4)
                act.wait_ge(row_evac, 4)
                act.dma_start(NF[:], norm_ffn[1].partition_broadcast(P)).then_inc(norm_row_in, 16)
            for m in range(NT):
                act.wait_ge(h_tr, layer * NT + m + 1)
                if m >= 2:
                    act.wait_ge(router_mm, layer * NT + m - 1)
                nc.scalar.activation(HTM[m % 2][:].rearrange("p c n -> p (c n)"), bank(2 * (m % 2), 2),
                                     ACT.Copy).then_inc(hT_ready, 1)
            act.wait_ge(router_mm, (layer + 1) * NT)
            nc.scalar.activation(SMALL[:, 0].rearrange("p m e -> p (m e)"), bank(4)[:, 0:P],
                                 ACT.Sigmoid).then_inc(logits_sig, 1)

            def xt_evac(s, par):
                act.wait_ge(xt_tr, s + (layer * MAX_SLOTS + 1))
                nc.scalar.activation(XT[par][:, 0:4, :].rearrange("p c n -> p (c n)"), bank(0),
                                     ACT.Copy).then_inc(xt_act, 1)

            def slot(s, par, more=True):
                b = layer * MAX_SLOTS
                act.wait_ge(gu_mm, s + (b + 1))
                act.wait_ge(he_ready, s + b)
                nc.scalar.activation(SG[:], bank(2)[:, 0:FF], ACT.Silu).then_inc(silu_g, 1)
                if more:
                    xt_evac(s + 1, 1 - par)

            xt_evac(0, 0)
            if layer == 0:
                act.wait_ge(gu_mm, 1)
                nc.scalar.activation(SG[:], bank(2)[:, 0:FF], ACT.Silu).then_inc(silu_g, 1)
                xt_evac(1, 1)
            else:
                slot(0, 0)
            with act.Fori(0, ALWAYS) as i:
                for k in range(2):
                    slot(2 * i + (1 + k), 1 - k)
            act.wait_ge(routed, layer + 1)
            used = slots_used(act)
            done = layer * MAX_SLOTS + 2
            with act.Fori(ALWAYS, PAIR_LOOPS) as i:
                with act.If(used > 2 * i):
                    for k in range(2):
                        slot(2 * i + (1 + k), 1 - k)
                with act.Else():
                    act.wait_ge(xt_act, 2 * i + done)
                    for sig in (silu_g, xt_act):
                        act.sem_inc(sig, 2)
            with act.If(used > 2 * PAIR_LOOPS):
                slot(MAX_SLOTS - 2, 1)
                slot(MAX_SLOTS - 1, 0, more=False)
            with act.Else():
                act.wait_ge(xt_act, 2 * PAIR_LOOPS + done)
                act.sem_inc(silu_g, 2)
                act.sem_inc(xt_act, 1)

            if layer == 0:
                for m in range(NT):
                    act.wait_ge(added, 2 * (m + 1))
                    squares(X[:, m, :], m, 2 * NT + m + 1)
                root(2)
                for ch in range(NC):
                    act.wait_ge(conv_tr, ch + 1)
                    nc.scalar.activation(HT[:, ch, 1:SEQ:2], bank(2 * (ch % 2)), ACT.Identity,
                                         scale=AC[:, 1, ch:ch + 1], bias=AC[:, 0, ch:ch + 1]).then_inc(hT_act, 1)

                def cin_evac(q, half, first=False):
                    b = 3 * half
                    act.wait_ge(cin_mm, q + 1)
                    if not first:
                        act.wait_ge(u_ready, q - 1)
                    nc.scalar.activation(CB[half][:], bank(b), ACT.Copy).then_inc(cb_ready, 1)
                    if not first:
                        act.wait_ge(z_ready, j_of(q, half))
                    nc.scalar.activation(BB[:, half * BANK:(half + 1) * BANK], bank(b + 2),
                                         ACT.Copy).then_inc(bb_ready, 1)

                def j_of(q, half):
                    return block_of[0]

                block_of = [0]
                for half in range(2):
                    cin_evac(half, half, first=True)
                with act.Fori(1, NC) as j:
                    block_of[0] = j
                    for half in range(2):
                        cin_evac(2 * j + half, half)
                row_evac_act(5, G1, 6)
                row_evac_act(6, SH2, 4)
                act.wait_ge(row_evac, 7)
                row_evac_act(8, G2, 4)

    @block.vector
    def _(dve):
        V = nc.vector
        count = [0]

        def link(ins):
            count[0] += 1
            ins.then_inc(dve_step, 1)
            dve.wait_ge(dve_step, count[0])

        def rstd(n):
            dve.wait_ge(sq_done, NT * (n + 1))
            V.tensor_scalar(VAR[:], SS[:], 1.0 / D, EPS, ALU.mult, ALU.add).then_inc(var_ready, 1)
            dve.wait_ge(sd_ready, n + 1)
            link(V.reciprocal(RS[:], SD[:]))
            link(V.tensor_tensor(RT[:], RS[:], RS[:], ALU.mult))
            link(V.tensor_tensor(RT[:], RT[:], VAR[:], ALU.mult))
            link(V.tensor_scalar(RT[:], RT[:], -0.5, 1.5, ALU.mult, ALU.add))
            link(V.tensor_tensor(RS[:], RS[:], RT[:], ALU.mult))

        rstd(0)
        for t in range(NT):
            link(V.tensor_scalar(XN[:, t, :], XN[:, t, :], RS[:, t:t + 1], None, ALU.mult))
        V.tensor_tensor(FB[:], XN[:, 0:4, :], XN[:, 4:8, :], ALU.subtract).then_inc(folds, 1)
        link(V.tensor_tensor(FA[:], XN[:, 0:4, :], XN[:, 4:8, :], ALU.add))
        V.tensor_tensor(FAB[:], FA[:, 0:2, :], FA[:, 2:4, :], ALU.subtract).then_inc(folds, 1)
        link(V.tensor_tensor(FAA[:], FA[:, 0:2, :], FA[:, 2:4, :], ALU.add))
        dve.wait_ge(folds, 2)
        V.tensor_tensor(FAAB[:], FAA[:, 0, :], FAA[:, 1, :], ALU.subtract).then_inc(folds, 1)
        V.tensor_tensor(FAAA[:], FAA[:, 0, :], FAA[:, 1, :], ALU.add).then_inc(folds, 1)

        def ada_block(dst, par, loads, step_at):
            dve.wait_ge(wa_in[par], loads * 16)
            for k in range(NC):
                ins = V.scalar_tensor_tensor(out=dst, in0=WA[par][:, k, :], scalar=SC[:, k:k + 1], in1=dst,
                                             op0=ALU.mult, op1=ALU.add)
                if k < NC - 1:
                    ins.then_inc(dve_step, 1)
                    dve.wait_ge(dve_step, step_at + (k + 1))
            ins.then_inc(wa_used, 1)

        def ada_first(b):
            ada_block(ACC[:, b * ADA_BLOCK:(b + 1) * ADA_BLOCK], b % 2, b // 2 + 1, count[0])
            count[0] += NC - 1

        dve.wait_ge(small_in, 16 * 8)
        dve.wait_ge(bias_in, 16)
        dve.wait_ge(silu_c, 1)
        dve.wait_ge(cols_mm, 1)
        link(V.tensor_tensor(AC[:, 0, :], bank(6)[:, 0:NC], BC[:, 0:NC], ALU.add))
        link(V.scalar_tensor_tensor(out=AC[:, 1, :], in0=bank(6)[:, NC:2 * NC], scalar=1.0, in1=BC[:, NC:2 * NC],
                                    op0=ALU.add, op1=ALU.add))
        V.tensor_tensor(AC[:, 1, :], AC[:, 1, :], NM[:, 0, :], ALU.mult).then_inc(cols_ready, 1)
        dve.wait_ge(cols_ready, 1)

        def pt_evac(dt):
            b = 3 * (dt % 2)
            dve.wait_ge(step1_mm, dt + 1)
            V.tensor_scalar(PT[:, dt, :, 256:512].rearrange("p s (k n) -> p k s n", k=2),
                            bank(b + 1).rearrange("p (k s n) -> p k s n", k=2, s=2),
                            AC[:, 1, dt:dt + 1], None, ALU.mult).then_inc(pt_dve, 1)
            link(V.tensor_scalar(PT[:, dt, :, 512:640], bank(b + 2)[:, 0:256].rearrange("p (s n) -> p s n", s=2),
                                 AC[:, 1, dt:dt + 1], None, ALU.mult))
            V.scalar_tensor_tensor(out=PT[:, dt, 0, 512:513], in0=AC[:, 0, dt:dt + 1],
                                   scalar=float(SEQ / np.sqrt(SEQ * GROUP)), in1=PT[:, dt, 0, 512:513],
                                   op0=ALU.mult, op1=ALU.add).then_inc(pt_dve, 1)

        def ef(g):
            dve.wait_ge(pt_act, 2 * g + 2)
            dve.wait_ge(pt_dve, 4 * g + 4)
            if g >= 2:
                dve.wait_ge(step2_mm, 2 * g - 2)
            a, b = PT[:, 2 * g], PT[:, 2 * g + 1]
            link(V.tensor_tensor(EF[g % 2][:, 0], a, b, ALU.add))
            V.tensor_tensor(EF[g % 2][:, 1], a, b, ALU.subtract).then_inc(ef_ready, 1)

        def mix_evac(ch):
            dve.wait_ge(vs_ready, ch + 1)
            dve.wait_ge(ft_act, ch + 1)
            u, v = bank(6), VS[:, ch % 2, :]
            V.tensor_tensor(FT[:, ch, 0:256], u[:, 0:256], v[:, 0:256], ALU.subtract)
            V.tensor_tensor(FT[:, ch, 512:640], u[:, 256:384], v[:, 256:384], ALU.subtract)
            V.tensor_tensor(FT[:, ch, 511:255:-1], u[:, 0:256], v[:, 0:256], ALU.add)
            V.tensor_tensor(FT[:, ch, 767:639:-1], u[:, 256:384], v[:, 256:384], ALU.add).then_inc(ft_dve, 1)

        b_ada_first = 2 * D // ADA_BLOCK
        for g in range(GROUPS):
            if g >= 2:
                for ch in (2 * g - 4, 2 * g - 3):
                    mix_evac(ch)
            for dt in (2 * g, 2 * g + 1):
                pt_evac(dt)
                ada_first(b_ada_first + dt)
            ef(g)
        for ch in range(4, NC):
            mix_evac(ch)
            ada_first(b_ada_first + 4 + ch)
        for b in range(b_ada_first + 12, N_ADA):
            ada_first(b)

        def residual(n, m, b):
            dve.wait_ge(y_mm, n + 1)
            if n >= 2:
                dve.wait_ge(x_ready, n - 1)
            link(V.tensor_tensor(XS[m % 2][:], bank(b, 2), G1, ALU.mult))
            V.tensor_tensor(X[:, m, :], X[:, m, :], XS[m % 2][:], ALU.add).then_inc(x_ready, 1)

        dve.wait_ge(row_evac, 1)
        for m in range(NT):
            dve.wait_ge(res_in[m], 16)
            residual(m, m, 2 * (m % 2))

        def scale_row(layer, n, b):
            dve.wait_ge(norm_row_in, 16 * (layer + 1))
            dve.wait_ge(rows_mm, n)
            V.scalar_tensor_tensor(out=GS2, in0=bank(b, 2), scalar=1.0, in1=NF[:], op0=ALU.add,
                                   op1=ALU.mult).then_inc(row_evac, 1)

        for layer in range(2):
            n0 = layer * NT
            rstd(1 + 2 * layer)
            if layer == 0:
                dve.wait_ge(row_evac, 2)
                scale_row(0, 3, 6)
            dve.wait_ge(row_evac, 4 * (layer + 1))
            for m in range(NT):
                if m >= 4:
                    dve.wait_ge(h_stored[m % 4], 16 * (2 * layer + 1))
                    dve.wait_ge(h_tr, n0 + m - 3)
                link(V.scalar_tensor_tensor(out=H[m % 4][:], in0=X[:, m, :], scalar=RS[:, m:m + 1], in1=GS2,
                                            op0=ALU.mult, op1=ALU.mult))
                V.tensor_tensor(H[m % 4][:], H[m % 4][:], SH2, ALU.add).then_inc(h_ready, 1)

            def t3(i):
                return SMALL[:, i]

            def g4(a):
                return a.rearrange("p m (g e) -> p (m g) e", g=EGROUPS)

            def tiny(i, n):
                return TINY[:, i, 0:n]

            def over_e(a, n):
                return a[:, :, None].to_broadcast([P, n, PER_GROUP])

            prio = K[:, C_PRIO:C_PRIO + PER_GROUP]
            MG = NT * EGROUPS
            dve.wait_ge(logits_sig, layer + 1)
            scores, biased, eq, rank, rest = t3(0), t3(1), t3(2), t3(3), t3(4)
            first, second, m1, m2 = t3(5), t3(6), t3(7), t3(8)
            link(V.tensor_tensor(biased, scores, RB[:, None, :].to_broadcast([P, NT, EXPERTS]), ALU.add))

            def first_of(dst, src, best, n, prio_b, shape):
                link(V.tensor_tensor(eq_of(n), src, best, ALU.is_equal))
                link(V.tensor_tensor(rank_of(n), eq_of(n), prio_b, ALU.mult))
                link(V.tensor_reduce(tiny(3, n), rank_of(n), X_AXIS, ALU.max))
                link(V.tensor_tensor(dst, rank_of(n), tiny(3, n)[:, :, None].to_broadcast(shape), ALU.is_equal))

            def eq_of(n):
                return g4(eq) if n == MG else tiny(4, MG).rearrange("p (m g) -> p m g", g=EGROUPS)

            def rank_of(n):
                return g4(rank) if n == MG else tiny(5, MG).rearrange("p (m g) -> p m g", g=EGROUPS)

            prio_in = prio[:, None, :].to_broadcast([P, MG, PER_GROUP])
            prio_groups = prio[:, None, :].to_broadcast([P, NT, EGROUPS])
            link(V.tensor_reduce(tiny(0, MG), g4(biased), X_AXIS, ALU.max))
            first_of(g4(first), g4(biased), over_e(tiny(0, MG), MG), MG, prio_in, [P, MG, PER_GROUP])
            link(V.scalar_tensor_tensor(out=rest, in0=first, scalar=-1e30, in1=biased, op0=ALU.mult, op1=ALU.add))
            link(V.tensor_reduce(tiny(1, MG), g4(rest), X_AXIS, ALU.max))
            first_of(g4(second), g4(rest), over_e(tiny(1, MG), MG), MG, prio_in, [P, MG, PER_GROUP])
            link(V.tensor_tensor(tiny(2, MG), tiny(0, MG), tiny(1, MG), ALU.add))
            sums = tiny(2, MG).rearrange("p (m g) -> p m g", g=EGROUPS)
            link(V.tensor_reduce(tiny(6, NT), sums, X_AXIS, ALU.max))
            in_group = tiny(7, MG)
            first_of(in_group.rearrange("p (m g) -> p m g", g=EGROUPS), sums,
                     tiny(6, NT)[:, :, None].to_broadcast([P, NT, EGROUPS]), NT, prio_groups, [P, NT, EGROUPS])
            link(V.tensor_tensor(g4(m1), g4(first), over_e(in_group, MG), ALU.mult))
            link(V.tensor_tensor(g4(m2), g4(second), over_e(in_group, MG), ALU.mult))
            both = t3(9)
            V.tensor_tensor(both, m1, m2, ALU.add).then_inc(mask_ready, 1)
            for i, mk in enumerate((m1, m2)):
                link(V.tensor_tensor(t3(10 + i), mk, scores, ALU.mult))
                link(V.tensor_reduce(tiny(8 + i, NT), t3(10 + i), X_AXIS, ALU.add))
            link(V.tensor_tensor(tiny(10, NT), tiny(8, NT), tiny(9, NT), ALU.add))
            link(V.reciprocal(tiny(11, NT), tiny(10, NT)))
            for i in range(TOP):
                link(V.tensor_tensor(tiny(8 + i, NT), tiny(8 + i, NT), tiny(11, NT), ALU.mult))
            dve.wait_ge(rank_mm, layer + 1)
            posn, total, before = t3(12), t3(13), t3(14)
            link(V.tensor_copy(posn.rearrange("p m e -> p (m e)"), bank(5)[:, 0:P]))
            link(V.tensor_copy(total.rearrange("p m e -> p (m e)"), bank(5)[:, P:2 * P]))
            link(V.memset(before[:, 0, :], 0.0))
            for m in range(1, NT):
                link(V.tensor_tensor(before[:, m, :], before[:, m - 1, :], total[:, m - 1, :], ALU.add))
            counts = tiny(12, EXPERTS)
            link(V.tensor_tensor(counts, before[:, NT - 1, :], total[:, NT - 1, :], ALU.add))
            over = t3(15).rearrange("p m e -> p (m e)").rearrange("p (e j) -> p e j", j=NT)
            link(V.tensor_tensor(over, counts[:, :, None].to_broadcast([P, EXPERTS, NT]),
                                 K[:, None, C_STEP:C_STEP + NT].to_broadcast([P, EXPERTS, NT]), ALU.is_gt))
            n_slots, start, end = tiny(13, EXPERTS), tiny(14, EXPERTS), tiny(15, EXPERTS)
            link(V.tensor_reduce(n_slots, over, X_AXIS, ALU.add))
            lower_e = SMALL[:, 16:18].rearrange("p a m e -> p (a m e)").rearrange("p (e k) -> p e k", k=EXPERTS)
            link(V.tensor_tensor(lower_e, n_slots[:, None, :].to_broadcast([P, EXPERTS, EXPERTS]),
                                 K[:, C_TRI:C_TRI + EXPERTS ** 2].rearrange("p (e k) -> p e k", k=EXPERTS), ALU.mult))
            link(V.tensor_reduce(start, lower_e, X_AXIS, ALU.add))
            link(V.tensor_tensor(end, start, n_slots, ALU.add))
            ended = SMALL[:, 18:23].rearrange("p a m e -> p (a m e)")[:, 0:MAX_SLOTS * EXPERTS].rearrange(
                "p (s e) -> p s e", e=EXPERTS)
            link(V.tensor_tensor(ended, end[:, None, :].to_broadcast([P, MAX_SLOTS, EXPERTS]),
                                 K[:, C_SLOT:C_SLOT + MAX_SLOTS][:, :, None].to_broadcast([P, MAX_SLOTS, EXPERTS]),
                                 ALU.is_le))
            link(V.tensor_reduce(tiny(16, MAX_SLOTS), ended, X_AXIS, ALU.add))
            link(V.tensor_scalar(SEID[:, 0:MAX_SLOTS], tiny(16, MAX_SLOTS), float(EXPERTS - 1), None, ALU.min))
            link(V.tensor_copy(SEID[:, MAX_SLOTS:MAX_SLOTS + 1], end[:, EXPERTS - 1:EXPERTS]))
            link(V.tensor_tensor(posn, posn, before, ALU.add))
            link(V.tensor_scalar(start, start, float(P), None, ALU.mult))
            link(V.tensor_tensor(posn, posn, start[:, None, :].to_broadcast([P, NT, EXPERTS]), ALU.add))
            for i, mk in enumerate((m1, m2)):
                link(V.tensor_tensor(t3(10 + i), mk, posn, ALU.mult))
                link(V.tensor_reduce(TINY[:, 17, i * NT:(i + 1) * NT], t3(10 + i), X_AXIS, ALU.add))
            pos = tiny(17, TOP * NT)
            POS = POSI[:].rearrange("p r m -> p (r m)")
            SLOTI, ROWI = TINY[:, 18, 0:TOP * NT].bitcast(u32), TINY[:, 19, 0:TOP * NT].bitcast(u32)
            link(V.tensor_copy(POS, pos))
            link(V.tensor_scalar(SLOTI, POS, 7, None, ALU.logical_shift_right))
            link(V.tensor_scalar(ROWI, POS, P - 1, None, ALU.bitwise_and))
            slot_f, row_f = tiny(20, TOP * NT), tiny(21, TOP * NT)
            link(V.tensor_copy(slot_f, SLOTI))
            link(V.tensor_copy(row_f, ROWI))
            A = TOP * NT
            V.tensor_tensor(ROWHOT[:], row_f[:, :, None].to_broadcast([P, A, P]),
                            K[:, None, C_ROW:C_ROW + P].to_broadcast([P, A, P]), ALU.is_equal).then_inc(hot_ready, 1)
            link(V.tensor_tensor(SLOTHOT[:, :, 1, :], slot_f[:, :, None].to_broadcast([P, A, MAX_SLOTS]),
                                 K[:, None, C_SLOT:C_SLOT + MAX_SLOTS].to_broadcast([P, A, MAX_SLOTS]), ALU.is_equal))
            for i in range(TOP):
                V.tensor_tensor(SLOTHOT[:, i * NT:(i + 1) * NT, 0, :], SLOTHOT[:, i * NT:(i + 1) * NT, 1, :],
                                K[:, C_TOKEN:C_TOKEN + NT][:, :, None].to_broadcast([P, NT, MAX_SLOTS]),
                                ALU.mult).then_inc(hot_ready, 1)
            dve.wait_ge(hot_ready, 5 * layer + 3)
            for i in range(TOP):
                V.tensor_tensor(SLOTHOT[:, i * NT:(i + 1) * NT, 1, :], SLOTHOT[:, i * NT:(i + 1) * NT, 1, :],
                                tiny(8 + i, NT)[:, :, None].to_broadcast([P, NT, MAX_SLOTS]),
                                ALU.mult).then_inc(hot_ready, 1)
            dve.wait_ge(table_mm, layer + 1)
            link(V.tensor_copy(TOKI[:], bank(6)[:, 0:MAX_SLOTS]))
            V.tensor_copy(WOF[:], bank(6)[:, MAX_SLOTS:2 * MAX_SLOTS]).then_inc(routed, 1)

            b = layer * MAX_SLOTS

            def heT_evac(s, par):
                dve.wait_ge(he_tr, s + (b + 1))
                V.tensor_copy(HET[par][:].rearrange("p f n -> p (f n)"), bank(3)[:, 0:FF]).then_inc(heT_ready, 1)

            def gated(s, par):
                dve.wait_ge(silu_g, s + (b + 1))
                V.tensor_tensor(HE[par][:], SG[:], bank(2)[:, FF:2 * FF], ALU.mult).then_inc(he_ready, 1)

            def xt_evac(s, par):
                dve.wait_ge(xt_tr, s + (b + 1))
                V.tensor_copy(XT[par][:, 4:8, :].rearrange("p c n -> p (c n)"), bank(1)).then_inc(xt_dve, 1)

            def y_evac(s, par, stored, never_stored=False):
                dve.wait_ge(yd_mm, s + (b + 1))
                if not never_stored:
                    dve.wait_ge(y_stored[par], stored * 16 + layer * SLOTS_OF[par] * 16)
                V.scalar_tensor_tensor(out=YO[par][:], in0=bank(4, 2), scalar=WOF[:, ds(s, 1)], in1=G2,
                                       op0=ALU.mult, op1=ALU.mult).then_inc(yo_ready, 1)

            def pair_slot(i, k):
                s, par = 2 * i + (1 + k), 1 - k
                heT_evac(s - 1, 1 - par)
                gated(s, par)
                xt_evac(s + 1, 1 - par)
                y_evac(s - 1, 1 - par, i)

            xt_evac(0, 0)
            gated(0, 0)
            xt_evac(1, 1)
            for s in (1, 2):
                heT_evac(s - 1, 1 - s % 2)
                gated(s, s % 2)
                xt_evac(s + 1, 1 - s % 2)
                y_evac(s - 1, 1 - s % 2, 0, never_stored=layer == 0)
            used = slots_used(dve)
            if layer == 0:
                dve.wait_ge(bias_in, 32)

            def ada_of(i, k):
                if layer == 0:
                    ada_block(ACC[:, ds((2 * i + (k - 2)) * ADA_BLOCK, ADA_BLOCK)], k, i + ADA_PAIRS,
                              (2 * i + (k - 2)) * (NC - 1) + count[0])

            def pair_if_used(i):
                with dve.If(used > 2 * i):
                    for k in range(2):
                        pair_slot(i, k)
                with dve.Else():
                    dve.wait_ge(yo_ready, 2 * i + b)
                    for sig in (heT_ready, he_ready, xt_dve, yo_ready):
                        dve.sem_inc(sig, 2)

            if layer == 0:
                with dve.Fori(1, ADA_MIXER // 2 + 1) as i:
                    for k in range(2):
                        ada_of(i, k)
                        pair_slot(i, k)
                count[0] += ADA_MIXER * (NC - 1)
            with dve.Fori(1 if layer else ADA_MIXER // 2 + 1, ALWAYS) as i:
                for k in range(2):
                    pair_slot(i, k)
            with dve.Fori(ALWAYS, PAIR_LOOPS) as i:
                pair_if_used(i)
            with dve.If(used > 2 * PAIR_LOOPS):
                for s in (MAX_SLOTS - 2, MAX_SLOTS - 1, MAX_SLOTS):
                    par = s % 2
                    heT_evac(s - 1, 1 - par)
                    if s < MAX_SLOTS:
                        gated(s, par)
                    if s + 1 < MAX_SLOTS:
                        xt_evac(s + 1, 1 - par)
                    y_evac(s - 1, 1 - par, (s - 1) // 2)
            with dve.Else():
                dve.wait_ge(yo_ready, 2 * PAIR_LOOPS + b)
                dve.sem_inc(heT_ready, 3)
                dve.sem_inc(he_ready, 2)
                dve.sem_inc(xt_dve, 1)
                dve.sem_inc(yo_ready, 3)

            if layer == 0:
                dve.wait_ge(cols_mm, 2)
                link(V.tensor_copy(AC[:, 0, :], bank(6)[:, 0:NC]))
                V.scalar_tensor_tensor(out=AC[:, 1, :], in0=bank(6)[:, NC:2 * NC], scalar=1.0, in1=NM[:, 1, :],
                                       op0=ALU.add, op1=ALU.mult).then_inc(cols_ready, 1)
                dve.wait_ge(cols_ready, 2)

            for q in range(TOP * NT):
                n = layer * TOP * NT + q
                dve.wait_ge(cg_in[q % 4], 16 * (4 * layer + q // 4 + 1))
                if q % 2:
                    dve.wait_ge(added, n)
                V.tensor_tensor(X[:, q // 2, :], X[:, q // 2, :], CG[q % 4][:], ALU.add).then_inc(added, 1)

            if layer == 0:
                rstd(2)
                for m in range(NT):
                    V.tensor_scalar(XN2[:, m, :], X[:, m, :], RS[:, m:m + 1], None, ALU.mult).then_inc(xn2_ready, 1)
                for ch in range(NC):
                    dve.wait_ge(conv_tr, ch + 1)
                    src = bank(2 * (ch % 2) + 1)
                    for at, (a, n, tok, step) in enumerate(((0, 2 * P, 2, 4), (2 * P, P, 4, 8), (3 * P, P, 0, 8))):
                        ins = V.tensor_scalar(HT[:, ch, tok:SEQ:step], src[:, a:a + n], AC[:, 1, ch:ch + 1],
                                              AC[:, 0, ch:ch + 1], ALU.mult, ALU.add)
                    ins.then_inc(hT_dve, 1)
                V.memset(U[:, 0:1], 0.0).then_inc(u_zero, 1)
                V.memset(U[:, SEQ + 1:SEQ + 2], 0.0).then_inc(u_zero, 1)
                dve.wait_ge(u_zero, 2)
                per_block = 3 + 2 * (NC - 1)
                with dve.Fori(0, NC) as j:
                    for half in range(2):
                        dve.wait_ge(cb_ready, 2 * j + (half + 1))
                        V.tensor_tensor(U[:, 1 + half * BANK:1 + (half + 1) * BANK], CB[half][:],
                                        bank(3 * half + 1), ALU.mult).then_inc(u_ready, 1)
                    dve.wait_ge(u_ready, 2 * j + 2)
                    at = j * per_block + count[0]
                    V.tensor_scalar(Z[:], U[:, 1:SEQ + 1], CW[:, 1, ds(j, 1)], None, ALU.mult).then_inc(dve_step, 1)
                    dve.wait_ge(dve_step, at + 1)
                    V.scalar_tensor_tensor(out=Z[:], in0=U[:, 0:SEQ], scalar=CW[:, 0, ds(j, 1)], in1=Z[:],
                                           op0=ALU.mult, op1=ALU.add).then_inc(dve_step, 1)
                    dve.wait_ge(dve_step, at + 2)
                    V.scalar_tensor_tensor(out=Z[:], in0=U[:, 2:SEQ + 2], scalar=CW[:, 2, ds(j, 1)], in1=Z[:],
                                           op0=ALU.mult, op1=ALU.add).then_inc(dve_step, 1)
                    dve.wait_ge(dve_step, at + 3)
                    dve.wait_ge(bb_ready, 2 * j + 2)
                    V.tensor_tensor(ZT[:, ds(j, 1), :].rearrange("p a n -> p (a n)"), Z[:], BB[:],
                                    ALU.mult).then_inc(z_ready, 1)
                    dve.wait_ge(z_ready, j + 1)
                    for k in range(2):
                        ada_block(ACC[:, ds((2 * j + (ADA_MIXER + k)) * ADA_BLOCK, ADA_BLOCK)], k,
                                  j + (ADA_PAIRS + ADA_MIXER // 2 + 1), j * per_block + (3 + k * (NC - 1) + count[0]))
                count[0] += per_block * NC
                dve.wait_ge(row_evac, 6)
                scale_row(1, 7, 6)
                for m in range(NT):
                    residual(NT + m, m, 2 * (m % 2))

    @block.tensor
    def _(pe):
        T = nc.tensor

        def first_columns():
            pe.wait_ge(silu_c, 1)
            for b in range(2 * D // ADA_BLOCK):
                pe.wait_ge(wa_in[b % 2], 16 * (b // 2 + 1))
                for j in range(2):
                    for k in range(NC):
                        ins = T.matmul(bank(6)[:, 2 * b + j:2 * b + j + 1], WA[b % 2][:, k, j * P:(j + 1) * P],
                                       SC[:, k:k + 1], start=k == 0, stop=k == NC - 1)
                ins.then_inc(wa_used, 1)
            T.matmul(bank(6)[:, 16:17], ident, SC[:, 0:1], start=True, stop=True).then_inc(cols_mm, 1)

        def columns():
            for j in range(2 * NC):
                ins = T.matmul(bank(6)[:, j:j + 1], ACC[:, j * P:(j + 1) * P], ones[:, 0:1], start=True, stop=True)
            ins.then_inc(cols_mm, 1)

        def row(piece, b):
            for h in range(2):
                ins = T.matmul(bank(b + h), ones, ACC[:, piece * D + h * BANK:piece * D + (h + 1) * BANK],
                               start=True, stop=True)
            ins.then_inc(rows_mm, 1)

        def step1(dt):
            b = 3 * (dt % 2)
            if dt >= 2:
                pe.wait_ge(pt_act, dt - 1)
                pe.wait_ge(pt_dve, 2 * dt - 2)
            cs = slice(dt * P, (dt + 1) * P)
            for t in range(4):
                T.matmul(bank(b), FB[:, t, cs], TB[:, t * 512:(t + 1) * 512], start=t == 0, stop=t == 3)
            for t in range(2):
                T.matmul(bank(b + 1)[:, 0:256], FAB[:, t, cs], TB[:, 2048 + t * 256:2304 + t * 256],
                         start=t == 0, stop=t == 1)
            T.matmul(bank(b + 1)[:, 256:512], FAAB[:, cs], TB[:, 2560:2816], start=True, stop=True)
            T.matmul(bank(b + 2)[:, 0:256], FAAA[:, cs], TB[:, 2816:3072], start=True, stop=True).then_inc(step1_mm, 1)

        def step2(g):
            pe.wait_ge(ef_ready, g + 1)
            for r in range(2):
                ch = 2 * g + r
                cos, sin, msin = (TB[:, 3072 + (3 * r + i) * P:3072 + (3 * r + i + 1) * P] for i in range(3))
                e = EF[g % 2][:, r]
                if ch == 0:
                    pe.wait_ge(cols_ready, 1)
                else:
                    pe.wait_ge(ft_act, ch)
                    pe.wait_ge(ft_dve, ch)
                T.matmul(bank(6)[:, 0:N_FOLD], cos, e[:, 0, 0:N_FOLD], start=True, stop=True)
                for i in range(2):
                    at = N_FOLD + i * P
                    T.matmul(bank(6 + i)[:, N_FOLD:BANK], cos, e[:, 0, at:at + P], start=True, stop=False)
                    T.matmul(bank(6 + i)[:, N_FOLD:BANK], msin, e[:, 1, at:at + P], start=False, stop=True)
                T.matmul(bank(7)[:, 0:N_FOLD], sin, e[:, 1, 0:N_FOLD], start=True, stop=True).then_inc(step2_mm, 1)

        pe.wait_ge(consts_in, 16)
        pe.wait_ge(tables_in, 16)
        pe.wait_ge(folds, 4)
        step1(0)
        step1(1)
        first_columns()
        step1(2)
        step1(3)
        step2(0)
        step1(4)
        step1(5)
        step2(1)
        step1(6)
        step1(7)
        step2(2)
        step2(3)
        pe.wait_ge(wa_used, 3 * D // ADA_BLOCK)
        pe.wait_ge(ft_dve, NC)
        pe.wait_ge(ft_act, NC)
        row(2, 6)
        pe.wait_ge(wf_in, 16 * GROUPS)
        for m in range(NT):
            b = 2 * (m % 2)
            if m >= 2:
                pe.wait_ge(x_ready, m - 1)
            for ch in range(NC):
                for h in range(2):
                    ins = T.matmul(bank(b + h), FT[:, ch, m * P:(m + 1) * P], WF[:, ch, h * BANK:(h + 1) * BANK],
                                   start=ch == 0, stop=ch == NC - 1)
            ins.then_inc(y_mm, 1)
        pe.wait_ge(wa_used, N_ADA)
        row(3, 4)
        pe.wait_ge(row_evac, 1)
        row(4, 6)
        pe.wait_ge(row_evac, 2)
        row(5, 4)

        for layer in range(2):
            n0, b0 = layer * NT, layer * MAX_SLOTS
            if layer == 0:
                pe.wait_ge(row_evac, 4)
            pe.wait_ge(x_ready, n0 + NT)

            def router(m):
                pe.wait_ge(hT_ready, n0 + m + 1)
                for ch in range(NC):
                    ins = T.matmul(bank(4)[:, m * EXPERTS:(m + 1) * EXPERTS], HTM[m % 2][:, ch, :], RW[:, ch, :],
                                   start=ch == 0, stop=ch == NC - 1)
                ins.then_inc(router_mm, 1)

            for m in range(NT):
                pe.wait_ge(h_ready, n0 + m + 1)
                if m >= 2:
                    pe.wait_ge(hT_ready, n0 + m - 1)
                for ch in range(NC):
                    ins = T.transpose(bank(2 * (m % 2), 2)[:, ch * P:(ch + 1) * P], H[m % 4][:, ch * P:(ch + 1) * P],
                                      ident)
                ins.then_inc(h_tr, 1)
                if m >= 1:
                    router(m - 1)
            router(NT - 1)
            both = SMALL[:, 9].rearrange("p m e -> p (m e)")
            pe.wait_ge(mask_ready, layer + 1)
            T.matmul(bank(5)[:, 0:P], lower, both, start=True, stop=True)
            T.matmul(bank(5)[:, P:2 * P], ones, both, start=True, stop=True).then_inc(rank_mm, 1)
            pe.wait_ge(hot_ready, 5 * (layer + 1))
            for a in range(TOP * NT):
                ins = T.matmul(bank(6)[:, 0:2 * MAX_SLOTS], ROWHOT[:, a, :], SLOTHOT[:, a].rearrange("p k s -> p (k s)"),
                               start=a == 0, stop=a == TOP * NT - 1)
            ins.then_inc(table_mm, 1)

            def transposes(s, par, nth):
                pe.wait_ge(gathered[layer][par], nth * 16)
                for ch in range(NC):
                    ins = T.transpose(bank(0, 2)[:, ch * P:(ch + 1) * P], XG[par][:, ch * P:(ch + 1) * P], ident)
                ins.then_inc(xt_tr, 1)

            def gate_up(s, par, nth):
                pe.wait_ge(xt_act, s + (b0 + 1))
                pe.wait_ge(xt_dve, s + (b0 + 1))
                pe.wait_ge(wgu_in[par], nth * 32 + layer * SLOTS_OF[par] * 32)
                for ch in range(NC):
                    ins = T.matmul(bank(2), XT[par][:, ch, :], WGU[par][:, ch, :], start=ch == 0, stop=ch == NC - 1)
                ins.then_inc(gu_mm, 1)

            def hidden_transposes(s, par):
                for f in range(FF // P):
                    ins = T.transpose(bank(3)[:, f * P:(f + 1) * P], HE[par][:, f * P:(f + 1) * P], ident)
                ins.then_inc(he_tr, 1)

            def down(s, par, nth):
                pe.wait_ge(heT_ready, s + (b0 + 1))
                pe.wait_ge(wd_in[par], nth * 16 + layer * SLOTS_OF[par] * 16)
                for h in range(2):
                    for f in range(FF // P):
                        ins = T.matmul(bank(4 + h), HET[par][:, f, :], WD[par][:, f, h * BANK:(h + 1) * BANK],
                                       start=f == 0, stop=f == FF // P - 1)
                ins.then_inc(yd_mm, 1)

            def slot(s, par, nth, prev_nth, next_nth, more=True, last=False):
                pe.wait_ge(he_ready, s + b0)
                if not last:
                    gate_up(s, par, nth)
                hidden_transposes(s - 1, 1 - par)
                if more:
                    transposes(s + 1, 1 - par, next_nth)
                pe.wait_ge(yo_ready, s + (b0 - 1))
                down(s - 1, 1 - par, prev_nth)

            pe.wait_ge(routed, layer + 1)
            transposes(0, 0, 1)
            gate_up(0, 0, 1)
            transposes(1, 1, 1)
            pe.wait_ge(he_ready, 1 + b0)
            gate_up(1, 1, 1)
            hidden_transposes(0, 0)
            transposes(2, 0, 2)
            down(0, 0, 1)
            slot(2, 0, 2, 1, 2)
            with pe.Fori(1, ALWAYS) as i:
                slot(2 * i + 1, 1, i + 1, i + 1, i + 2)
                slot(2 * i + 2, 0, i + 2, i + 1, i + 2)
            used = slots_used(pe)
            with pe.Fori(ALWAYS, PAIR_LOOPS) as i:
                with pe.If(used > 2 * i):
                    slot(2 * i + 1, 1, i + 1, i + 1, i + 2)
                    slot(2 * i + 2, 0, i + 2, i + 1, i + 2)
                with pe.Else():
                    pe.wait_ge(yd_mm, 2 * i + b0)
                    for sig in (xt_tr, gu_mm, he_tr, yd_mm):
                        pe.sem_inc(sig, 2)
            n = PAIR_LOOPS
            with pe.If(used > 2 * n):
                slot(MAX_SLOTS - 2, 1, n + 1, n + 1, n + 2)
                slot(MAX_SLOTS - 1, 0, n + 2, n + 1, 0, more=False)
                slot(MAX_SLOTS, 1, 0, n + 2, 0, more=False, last=True)
            with pe.Else():
                pe.wait_ge(yd_mm, 2 * n + b0)
                pe.sem_inc(xt_tr, 1)
                pe.sem_inc(gu_mm, 2)
                pe.sem_inc(he_tr, 3)
                pe.sem_inc(yd_mm, 3)

            if layer == 0:
                pe.wait_ge(wa_used, N_ADA + ADA_MIXER)
                columns()
                pe.wait_ge(xn2_ready, NT)
                for ch in range(NC):
                    if ch >= 2:
                        pe.wait_ge(hT_act, ch - 1)
                        pe.wait_ge(hT_dve, ch - 1)
                    for m in range(NT):
                        ins = T.transpose(bank(2 * (ch % 2), 2)[:, m * P:(m + 1) * P],
                                          XN2[:, m, ch * P:(ch + 1) * P], ident)
                    ins.then_inc(conv_tr, 1)
                pe.wait_ge(hT_act, NC)
                pe.wait_ge(hT_dve, NC)

                def cin(j_plus, par, half, wait_free):
                    if wait_free is not None:
                        pe.wait_ge(u_ready, wait_free)
                        pe.wait_ge(bb_ready, wait_free)
                    for slot_b, s in enumerate((1, 2, 0)):
                        for ch in range(NC):
                            ins = T.matmul(bank(3 * half + slot_b), WIN[par][:, ch, s, :],
                                           HT[:, ch, half * BANK:(half + 1) * BANK], start=ch == 0, stop=ch == NC - 1)
                    ins.then_inc(cin_mm, 1)

                for j in range(2):
                    pe.wait_ge(win_in[j], 48)
                    for half in range(2):
                        cin(j, j, half, None if j == 0 else half + 1)
                with pe.Fori(1, NC // 2) as i:
                    for k in range(2):
                        pe.wait_ge(win_in[k], i * 48 + 48)
                        for half in range(2):
                            cin(None, k, half, 4 * i + (2 * k + half - 1))
                pe.wait_ge(wa_used, 2 * N_ADA)
                row(2, 6)
                pe.wait_ge(bb_ready, 2 * NC)
                row(3, 4)
                pe.wait_ge(row_evac, 5)
                row(4, 6)
                pe.wait_ge(row_evac, 6)
                row(5, 4)
                pe.wait_ge(z_ready, NC)
                for m, (first, step) in enumerate(TILES):
                    b = 2 * (m % 2)
                    if m >= 2:
                        pe.wait_ge(x_ready, NT + m - 1)
                    last = first + (P - 1) * step + 1
                    for ch in range(NC):
                        if m == 0 and ch % 2 == 0:
                            pe.wait_ge(wout_in[ch // 2], 16)
                        for h in range(2):
                            ins = T.matmul(bank(b + h), ZT[:, ch, first:last:step], WOUT[:, ch, h * BANK:(h + 1) * BANK],
                                           start=ch == 0, stop=ch == NC - 1)
                    ins.then_inc(y_mm, 1)

    top.close()


INPUTS = ["x", "c", "w_ada", "b_ada", "norm_mix", "norm_ffn", "fourier_w_out", "conv_w_in", "conv_w", "conv_w_out",
          "router_w", "router_bias", "moe_w_gate", "moe_w_up", "moe_w_down"]


def kernel(**inputs):
    import numpy as _np
    import concourse.bacc as _bacc
    from concourse import mybir as _mybir
    from concourse.bass_utils import run_bass_kernel_spmd as _run

    nc = _bacc.Bacc("TRN2", target_bir_lowering=False, num_devices=1)
    arrays, args = {}, []
    given = [(name, inputs[name]) for name in INPUTS] + [("tables", dft_tables()), ("constants", shape_constants())]
    for name, value in given:
        a = _np.ascontiguousarray(value)
        arrays[f"in_{name}_dram"] = a
        args.append(nc.dram_tensor(f"in_{name}_dram", a.shape, _mybir.dt.from_np(a.dtype), kind="ExternalInput").ap())
    out = nc.dram_tensor("out_0_dram", (1, SEQ, D), _mybir.dt.float32, kind="ExternalOutput").ap()
    backbone(nc, *args, out)
    r = _run(nc, [arrays], core_ids=[0])
    return r.results[0]["out_0_dram"]
```

```python
import numpy as np
from contextlib import ExitStack

import concourse.bass as bass
from concourse import mybir

P = 128
SEQ, D = 1024, 1024
NT = SEQ // P
NC = D // P
BANK = 512
GROUPS, GROUP = 4, 256
EXPERTS, EGROUPS, PER_GROUP, TOP = 16, 4, 4, 2
FF = 256
PAIRS = SEQ * TOP
MAX_SLOTS = (PAIRS + EXPERTS * (P - 1)) // P
ADA = 6 * D
ADA_BLOCK = 256
N_ADA = ADA // ADA_BLOCK
EPS = 1e-6
TILES = [(1, 2), (257, 2), (513, 2), (769, 2), (2, 4), (514, 4), (4, 8), (0, 8)]
N_FOLD = 384
N_FREQ = 640
N_TABLE = 4 * 512 + 2 * 256 + 256 + 256 + 6 * P


def dft_tables():
    n = np.arange(512)[:, None]

    def pos(rows, k):
        a = 2 * np.pi * ((n[:rows] * k[None, :]) % SEQ) / SEQ
        t = np.concatenate([np.cos(a), np.sin(a)], 1) / np.sqrt(SEQ * GROUP)
        return t.reshape(rows // P, P, -1).transpose(1, 0, 2).reshape(P, -1)

    j = np.arange(256)
    parts = [pos(512, 2 * j + 1), pos(256, 4 * j[:128] + 2), pos(128, 8 * j[:128] + 4), pos(128, 8 * j[:128])]
    d = np.arange(P)[:, None]
    for parity in range(2):
        a = 2 * np.pi * ((d * (2 * j[None, :128] + parity)) % GROUP) / GROUP
        parts += [np.cos(a), np.sin(a), -np.sin(a)]
    return np.concatenate(parts, 1).astype(np.float32)


C_IDENT, C_ONES, C_LOWER, C_ROW = 0, 128, 256, 384
C_PRIO, C_TRI, C_STEP, C_TOKEN, C_SLOT = 512, 516, 772, 780, 788
N_CONST = 788 + 40


def shape_constants():
    t = np.zeros((P, N_CONST), np.float32)
    i = np.arange(P)
    t[:, C_IDENT:C_IDENT + P] = np.eye(P)
    t[:, C_ONES:C_ONES + P] = 1
    t[:, C_LOWER:C_LOWER + P] = i[:, None] < i[None, :]
    t[:, C_ROW:C_ROW + P] = i
    t[:, C_PRIO:C_PRIO + PER_GROUP] = PER_GROUP - np.arange(PER_GROUP)
    e = np.arange(EXPERTS)
    t[:, C_TRI:C_TRI + EXPERTS ** 2] = (e[None, :] < e[:, None]).reshape(-1)
    t[:, C_STEP:C_STEP + NT] = P * np.arange(NT)
    t[:, C_TOKEN:C_TOKEN + NT] = i[:, None] + P * np.arange(NT)
    t[:, C_SLOT:C_SLOT + 40] = np.arange(40)
    return t


def backbone(nc, x, c, w_ada, b_ada, norm_mix, norm_ffn, fourier_w_out, conv_w_in, conv_w, conv_w_out,
             router_w, router_bias, moe_w_gate, moe_w_up, moe_w_down, tables, constants, out):
    f32, f32r, i32, u32 = mybir.dt.float32, mybir.dt.float32r, mybir.dt.int32, mybir.dt.uint32
    ALU, ACT, X_AXIS = mybir.AluOpType, mybir.ActivationFunctionType, mybir.AxisListType.X
    top = ExitStack()
    ds = bass.ds

    def sem(name):
        return top.enter_context(nc.semaphore(name))

    def width(shape):
        n = 4
        for k in shape[1:]:
            n *= k
        return n

    class Region:

        def __init__(self, start):
            self.at = start

        def put(self, name, shape, dt=f32):
            t = nc.alloc_sbuf_tensor_at(name, shape, dt, offset=self.at)
            self.at += (width(shape) + 31) // 32 * 32
            return t

    x_rows, out_rows = x[0], out[0]

    arena = top.enter_context(nc.sbuf_tensor("arena", [P, (nc.sbuf_bytes_remaining - 1024) // 4], f32))
    base = (nc.sbuf_base - width(arena.shape) + 31) // 32 * 32
    keep = Region(base)
    X = keep.put("X", [P, NT, D])
    XS = [keep.put(f"XS{i}", [P, D]) for i in range(2)]
    ROWS = keep.put("ROWS", [P, 4, D])
    G1, GS2, SH2, G2 = (ROWS[:, i, :] for i in range(4))
    K = keep.put("K", [P, N_CONST])
    ident, ones, lower = (K[:, a:a + P] for a in (C_IDENT, C_ONES, C_LOWER))
    RW = keep.put("RW", [P, NC, EXPERTS])
    RB = keep.put("RB", [P, EXPERTS])
    CW = keep.put("CW", [P, 3, NC])
    CC = keep.put("CC", [P, NC])
    SC = keep.put("SC", [P, NC])
    NM = keep.put("NM", [P, 2, NC])
    AC = keep.put("AC", [P, 3, NC])
    SHS = keep.put("SHS", [P, 2, GROUPS])
    SS, VAR, SD, RS, RT = (keep.put(n, [P, NT]) for n in ("SS", "VAR", "SD", "RS", "RT"))
    TOKI = keep.put("TOKI", [P, MAX_SLOTS], u32)
    WOF = keep.put("WOF", [P, MAX_SLOTS])
    SEID = keep.put("SEID", [P, MAX_SLOTS + 1], i32)
    POSI = keep.put("POSI", [P, TOP, NT], u32)
    SQ = keep.put("SQ", [P, D])
    ada_at = keep.at
    ACC = keep.put("ACC", [P, ADA])
    WA = [keep.put(f"WA{i}", [P, NC, ADA_BLOCK]) for i in range(2)]
    fourier_at = keep.at
    phase = keep.at

    PT = Region(base).put("PT", [P, NC, 2, N_FREQ])
    r = Region(base + width(PT.shape))
    FAB = r.put("FAB", [P, 2, D])
    FAA = r.put("FAA", [P, 2, D])
    r = Region(fourier_at)
    XN = r.put("XN", [P, NT, D])
    fold_at = r.at
    FB = r.put("FB", [P, 4, D])
    fa_at = r.at
    FA = r.put("FA", [P, 4, D])
    tables_at = r.at
    TB = r.put("TB", [P, N_TABLE])
    ef_at = r.at
    EF = [r.put(f"EF{i}", [P, 2, 2, N_FREQ]) for i in range(2)]
    assert r.at <= base + width(arena.shape) - 32, (r.at - base, width(arena.shape))
    r = Region(fa_at)
    FAAB = r.put("FAAB", [P, D])
    FAAA = r.put("FAAA", [P, D])
    WAE = Region(ef_at).put("WAE", [P, 2, NC, ADA_BLOCK])
    FT = Region(fourier_at).put("FT", [P, NC, SEQ])
    WF = Region(fold_at).put("WF", [P, NC, D])
    VS = Region(ada_at - width(SQ.shape)).put("VS", [P, 2, N_FOLD])

    ST = Region(ada_at - width(SQ.shape)).put("ST", [EXPERTS, SEQ])
    r = Region(phase)
    WGU = [r.put(f"WGU{i}", [P, NC, 2 * FF]) for i in range(2)]
    WD = [r.put(f"WD{i}", [P, FF // P, D]) for i in range(2)]
    XG = [r.put(f"XG{i}", [P, D]) for i in range(2)]
    XT = [r.put(f"XT{i}", [P, NC, P]) for i in range(2)]
    YO = [r.put(f"YO{i}", [P, D]) for i in range(2)]
    HE = [r.put(f"HE{i}", [P, FF]) for i in range(2)]
    HET = [r.put(f"HET{i}", [P, FF // P, P]) for i in range(2)]
    SG = r.put("SG", [P, FF])
    NF0 = Region(tables_at).put("NF0", [P, D])
    r = Region(ada_at)
    H = [r.put(f"H{i}", [P, D]) for i in range(4)]
    HTM = [r.put(f"HTM{i}", [P, NC, P]) for i in range(2)]
    r = Region(phase)
    SMALL = r.put("SMALL", [P, 24, NT, EXPERTS])
    TINY = r.put("TINY", [P, 24, 40])
    ROWHOT = r.put("ROWHOT", [P, TOP * NT, P])
    SLOTHOT = r.put("SLOTHOT", [P, TOP * NT, 2, MAX_SLOTS])
    assert r.at <= base + width(arena.shape) - 32, (r.at - base, width(arena.shape))
    CG = [Region(phase + 4096 * i).put(f"CG{i}", [P, D]) for i in range(8)]

    r = Region(phase)
    HTH = r.put("HTH", [P, NC, SEQ], f32r)
    HTL = r.put("HTL", [P, NC, SEQ], f32r)
    zt_at = r.at
    ZT = r.put("ZT", [P, NC, SEQ])
    u_at = r.at
    U = r.put("U", [P, SEQ + 2])
    assert r.at <= base + width(arena.shape) - 32, (r.at - base, width(arena.shape))
    NF = Region(u_at).put("NF", [P, D])
    rows_at = base + width(X.shape) + 2 * width(XS[0].shape)
    r = Region(rows_at)
    WINL = [r.put(f"WINL{i}", [P, NC, P], f32r) for i in range(2)]
    WINH = [r.put(f"WINH{i}", [P, NC, P], f32r) for i in range(2)]
    r = Region(rows_at)
    WINR = [r.put(f"WINR{i}", [P, NC, P]) for i in range(2)]
    r = Region(ada_at - width(SQ.shape))
    CB = [r.put(f"CB{i}", [P, BANK]) for i in range(2)]
    r = Region(base + width(X.shape))
    HTF = [r.put(f"HTF{i}", [P, SEQ]) for i in range(2)]
    r = Region(base + width(X.shape))
    Z, BB = r.put("Z", [P, SEQ]), r.put("BB", [P, SEQ])
    XN2 = Region(zt_at).put("XN2", [P, NT, D])
    WOR = Region(phase).put("WOR", [P, NC, D])
    r = Region(phase)
    WOL, WOH = r.put("WOL", [P, NC, D], f32r), r.put("WOH", [P, NC, D], f32r)
    r = Region(ada_at + width(ACC.shape))
    ZH = [r.put(f"ZH{i}", [P, NC, P], f32r) for i in range(2)]
    ZL = [r.put(f"ZL{i}", [P, NC, P], f32r) for i in range(2)]

    PS = top.enter_context(nc.psum_tensor("PS", [P, 8, BANK], f32))

    def bank(i, n=1):
        return PS[:, i:i + n, :].rearrange("p b n -> p (b n)")

    h_dram = [nc.dram_tensor(f"h_dram{i}", [SEQ, D], f32, kind="Internal").ap() for i in range(2)]
    y_dram = [nc.dram_tensor(f"y_dram{i}", [MAX_SLOTS * P, D], f32, kind="Internal").ap() for i in range(2)]

    consts_in, small_in, c_in, tables_in = sem("consts_in"), sem("small_in"), sem("c_in"), sem("tables_in")
    bias_in, norm_row_in, out_done = (
        sem(n) for n in ("bias_in", "norm_row_in", "out_done"))
    wf_in = [sem(f"wf_in{i}") for i in range(GROUPS)]
    wout_in = [sem(f"wout_in{i}") for i in range(4)]
    x_in = [sem(f"x_in{i}") for i in range(4)]
    res_in = [sem(f"res_in{i}") for i in range(NT)]
    wa_in = [sem(f"wa_in{i}") for i in range(4)]
    win_in = [sem(f"win_in{i}") for i in range(2)]
    h_stored = [sem(f"h_stored{i}") for i in range(4)]
    gathered = [[sem(f"gathered{layer}_{i}") for i in range(2)] for layer in range(2)]
    wgu_in = [sem(f"wgu_in{i}") for i in range(2)]
    wd_in = [sem(f"wd_in{i}") for i in range(2)]
    y_stored = [sem(f"y_stored{i}") for i in range(2)]
    cg_in = [sem(f"cg_in{i}") for i in range(8)]
    (y_filled, scores_T, pt_scaled, rs_ready, scaled, acc_clear, wa_used, silu_c, sq_done, var_ready, sd_ready, folds, cols_mm, cols_ready, step1_mm, pt_act,
     pt_dve, ef_ready, step2_mm, vs_ready, ft_act, ft_dve, rows_mm, row_evac, y_mm, x_ready, h_ready, h_tr,
     hT_ready, router_mm, scores_tr, mask_ready, rank_mm, hot_ready, table_mm, routed, xt_tr, xt_act, xt_dve,
     gu_mm, silu_g, he_ready, he_tr, heT_ready, yd_mm, yo_ready, added, xn2_ready, conv_tr, hT_act,
     win_free, wout_high, wout_low, z_high, z_low, win_high, win_low, hT_high, hT_dve, cin_mm, cb_ready, bb_ready, u_ready, z_ready, u_zero) = (
        sem(n) for n in ("y_filled scores_T pt_scaled rs_ready scaled acc_clear wa_used silu_c sq_done var_ready sd_ready folds cols_mm cols_ready step1_mm "
                         "pt_act pt_dve ef_ready step2_mm vs_ready ft_act ft_dve rows_mm row_evac y_mm x_ready "
                         "h_ready h_tr hT_ready router_mm scores_tr mask_ready rank_mm hot_ready table_mm routed "
                         "xt_tr xt_act xt_dve gu_mm silu_g he_ready he_tr heT_ready yd_mm yo_ready added "
                         "xn2_ready conv_tr hT_act win_free wout_high wout_low z_high z_low win_high win_low hT_high hT_dve cin_mm cb_ready bb_ready u_ready z_ready u_zero").split())
    act_step, dve_step = sem("act_step"), sem("dve_step")

    block = top.enter_context(nc.Block())
    PAIR_LOOPS = (MAX_SLOTS - 3) // 2
    PARTS = (1, 2, 0)
    NORMS = ((0, 1, 2, 3), (4, 5), (6,), (7,))
    ADA_MIXER = 2 * D // ADA_BLOCK
    ADA_EARLY = ADA_MIXER // 4
    ADA_LOADS = ADA_EARLY + (N_ADA - ADA_MIXER) // 2
    WA_ALL = [WA[0][:], WA[1][:], WAE[:, 0], WAE[:, 1]]
    ALWAYS = PAIRS // P // 2
    SLOTS_OF = [(MAX_SLOTS + 1) // 2, MAX_SLOTS // 2]

    def ada_columns(layer, b):
        return w_ada[layer].rearrange("(p k) n -> p k n", k=NC)[:, :, ds(b * ADA_BLOCK, ADA_BLOCK)]

    def load_ada(sp, layer, b, par):
        sp.dma_start(WA_ALL[par], ada_columns(layer, b)).then_inc(wa_in[par], 16)

    def tile_of(t, m):
        first, step = TILES[m]
        return t[:, :, first:first + (P - 1) * step + 1:step]

    def fill_unused(sp, layer):
        rows = y_dram[layer].rearrange("s (c n) -> s c n", n=P)
        with sp.Fori(PAIRS // P, MAX_SLOTS) as s:
            sp.dma_start(rows[ds(s * P, P), :, :], ones[:, None, :].to_broadcast([P, NC, P])).then_inc(y_filled, 16)

    def slots_used(engine):
        return engine.value_load(SEID[0:1, MAX_SLOTS:MAX_SLOTS + 1], min_val=PAIRS // P, max_val=MAX_SLOTS)

    @block.sync
    def _(sp):
        sp.dma_start(K[:], constants).then_inc(consts_in, 16)
        xv = x_rows.rearrange("(t p) d -> p t d", p=P)
        for q in range(4):
            sp.dma_start(XN[:, q, :], xv[:, q, :]).then_inc(x_in[q], 16)
            sp.dma_start(XN[:, q + 4, :], xv[:, q + 4, :]).then_inc(x_in[q], 16)
        sp.dma_start(TB[:], tables).then_inc(tables_in, 16)
        for b in range(ADA_MIXER):
            if b >= 4:
                sp.wait_ge(wa_used, b - 3)
            load_ada(sp, 0, b, b % 4)
        for par in range(2):
            sp.wait_ge(wa_used, ADA_MIXER - 3 + par)
            load_ada(sp, 0, ADA_MIXER + par, par)
        with sp.Fori(ADA_MIXER // 2 + 1, N_ADA // 2) as i:
            for par in range(2):
                sp.wait_ge(wa_used, 2 * i + par - 1)
                load_ada(sp, 0, 2 * i + par, par)
        sp.wait_ge(consts_in, 16)
        fill_unused(sp, 0)

        def expert_of(s):
            return sp.value_load(SEID[0:1, ds(s, 1)], min_val=0, max_val=EXPERTS - 1)

        def load_gate_up(layer, e, par):
            for j, w in enumerate((moe_w_gate, moe_w_up)):
                src = w[layer].rearrange("e d f -> (e d) f")[ds(e * D, D), :].rearrange("(c p) f -> p c f", p=P)
                sp.dma_start(WGU[par][:, :, j * FF:(j + 1) * FF], src).then_inc(wgu_in[par], 16)

        def load_down(layer, e, par):
            src = moe_w_down[layer].rearrange("e f d -> (e f) d")[ds(e * FF, FF), :].rearrange("(f p) d -> p f d", p=P)
            sp.dma_start(WD[par][:], src).then_inc(wd_in[par], 16)

        def store_y(layer, s, par):
            sp.dma_start(y_dram[layer][ds(s * P, P), :], YO[par][:]).then_inc(y_stored[par], 16)

        def slot(layer, s, par, first=False, load2=True, load1=True):
            b = layer * MAX_SLOTS
            e2 = expert_of(s + 2) if load2 else None
            e1 = expert_of(s + 1) if load1 else None
            if load2:
                sp.wait_ge(gu_mm, s + (b + 1))
                load_gate_up(layer, e2, par)
            if load1:
                if not first:
                    sp.wait_ge(yd_mm, s + b)
                load_down(layer, e1, 1 - par)
            if not first:
                sp.wait_ge(yo_ready, s + b)
                store_y(layer, s - 1, 1 - par)

        for layer in range(2):
            for m in range(NT):
                sp.wait_ge(h_ready, layer * NT + m + 1)
                sp.dma_start(h_dram[layer][m * P:(m + 1) * P, :], H[m % 4][:]).then_inc(h_stored[m % 4], 16)
            sp.wait_ge(routed, layer + 1)
            used = slots_used(sp)
            sp.wait_ge(y_filled, 16 * (MAX_SLOTS - PAIRS // P) * (layer + 1))
            load_gate_up(layer, expert_of(0), 0)
            load_gate_up(layer, expert_of(1), 1)
            load_down(layer, expert_of(0), 0)
            slot(layer, 0, 0, first=True)

            def pair(i):
                for k in range(2):
                    slot(layer, 2 * i + (1 + k), 1 - k)

            def skip_pair(i):
                for par in range(2):
                    n = layer * SLOTS_OF[par]
                    sp.wait_ge(wgu_in[par], i * 32 + (2 - par + n) * 32)
                    sp.sem_inc(wgu_in[par], 32)
                    sp.wait_ge(wd_in[par], i * 16 + (1 + n) * 16)
                    sp.sem_inc(wd_in[par], 16)
                    sp.wait_ge(y_stored[par], i * 16 + n * 16)
                    sp.sem_inc(y_stored[par], 16)

            def pair_if_used(i):
                with sp.If(used > 2 * i):
                    pair(i)
                with sp.Else():
                    skip_pair(i)

            if layer == 0:
                with sp.Fori(0, ADA_MIXER // 2) as i:
                    for k in range(2):
                        slot(layer, 2 * i + (1 + k), 1 - k)
                        sp.wait_ge(wa_used, 2 * i + (N_ADA + k - 1))
                        load_ada(sp, 1, 2 * i + k, k)
            with sp.Fori(0 if layer else ADA_MIXER // 2, ALWAYS) as i:
                pair(i)
            with sp.Fori(ALWAYS, PAIR_LOOPS) as i:
                pair_if_used(i)
            with sp.If(used > 2 * PAIR_LOOPS):
                slot(layer, MAX_SLOTS - 2, 1, load2=False)
                slot(layer, MAX_SLOTS - 1, 0, load2=False, load1=False)
                slot(layer, MAX_SLOTS, 1, load2=False, load1=False)
            with sp.Else():
                sp.wait_ge(wd_in[0], (PAIR_LOOPS + 1 + layer * SLOTS_OF[0]) * 16)
                sp.sem_inc(wd_in[0], 16)
                for par in range(2):
                    sp.wait_ge(y_stored[par], (PAIR_LOOPS + layer * SLOTS_OF[par]) * 16)
                    sp.sem_inc(y_stored[par], 16 * (SLOTS_OF[par] - PAIR_LOOPS))
            if layer == 0:
                def load_win(j, part, par):
                    src = conv_w_in[0].rearrange("(c p) (s n) -> p c s n", p=P, s=3)[:, :, part, ds(j * P, P)]
                    sp.dma_start(WINR[par][:], src).then_inc(win_in[par], 16)

                def load_ada_pair(j):
                    for k in range(2):
                        sp.wait_ge(wa_used, 2 * j + (N_ADA + ADA_MIXER + k - 1))
                        load_ada(sp, 1, 2 * j + (ADA_MIXER + k), k)

                load_ada_pair(0)
                sp.wait_ge(added, 2 * NT - 4)
                load_win(0, PARTS[0], 0)
                load_win(0, PARTS[1], 1)
                fill_unused(sp, 1)
                sp.wait_ge(cin_mm, 1)
                load_win(0, PARTS[2], 0)
                for n in range(3):
                    sp.wait_ge(cin_mm, n + 2)
                    load_win(1, PARTS[n], (n + 1) % 2)
                with sp.Fori(1, NC // 2) as i:
                    for k in range(2):
                        for n in range(3):
                            sp.wait_ge(cin_mm, 6 * i + (3 * k + n - 1))
                            sp.sem_inc(win_free, 1)
                            load_win(2 * i + k, PARTS[n], (k + n) % 2)
                            if n == 0:
                                load_ada_pair(2 * i + (k - 1))
                load_ada_pair(NC - 1)
                sp.wait_ge(cin_mm, 3 * NC)
                for q in range(4):
                    sp.dma_start(WOR[:, 2 * q:2 * q + 2, :],
                                 conv_w_out[0, 2 * q * P:2 * (q + 1) * P, :].rearrange("(j p) n -> p j n", p=P)
                                 ).then_inc(wout_in[q], 16)
        for m, (first, step) in enumerate(TILES):
            sp.wait_ge(added, 2 * NT + 2 * (m + 1))
            sp.dma_start(out_rows[ds(first, P, step=step), :], X[:, m, :]).then_inc(out_done, 16)
        sp.wait_ge(out_done, 16 * NT)

    @block.gpsimd
    def _(pool):
        def bias_row(layer):
            pool.memset(ACC[:], 0.0).then_inc(acc_clear, 1)
            pool.wait_ge(acc_clear, layer + 1)
            pool.dma_start(ACC[0:1, :], b_ada[layer:layer + 1, :]).then_inc(bias_in, 16)

        bias_row(0)

        def gather(layer, s, par):
            pool.indirect_dma_start(out=XG[par][:], out_offset=None, in_=h_dram[layer],
                                    in_offset=bass.IndirectOffsetOnAxis(ap=TOKI[:, s:s + 1], axis=0)
                                    ).then_inc(gathered[layer][par], 16)

        def slot(layer, s, par):
            pool.wait_ge(xt_tr, s + (layer * MAX_SLOTS + 1))
            gather(layer, s + 2, par)

        for layer in range(2):
            for i in range(4):
                pool.wait_ge(h_stored[i], 32 * (layer + 1))
            pool.wait_ge(routed, layer + 1)
            used = slots_used(pool)
            gather(layer, 0, 0)
            gather(layer, 1, 1)
            if layer == 0:
                bias_row(1)
            for i in range(PAIR_LOOPS + 1):
                slots = range(2 * i, min(2 * i + 2, MAX_SLOTS - 2))
                if i < ALWAYS:
                    for s in slots:
                        slot(layer, s, s % 2)
                    continue
                with pool.If(used > 2 * i):
                    for s in slots:
                        slot(layer, s, s % 2)
            for par in range(2):
                pool.wait_ge(y_stored[par], 16 * SLOTS_OF[par] * (layer + 1))
            for q in range(TOP * NT):
                n = layer * TOP * NT + q
                if q >= 8:
                    pool.wait_ge(added, n - 7)
                pool.indirect_dma_start(out=CG[q % 8][:], out_offset=None, in_=y_dram[layer],
                                        in_offset=bass.IndirectOffsetOnAxis(ap=POSI[:, q % 2, q // 2:q // 2 + 1], axis=0)
                                        ).then_inc(cg_in[q % 8], 16)

    @block.scalar
    def _(act):
        count = [0]

        def link(ins):
            count[0] += 1
            ins.then_inc(act_step, 1)
            act.wait_ge(act_step, count[0])

        with nc.allow_non_contiguous_dma(reason="vectors by channel, a few KB"):
            act.dma_start(CC[:], c[0].rearrange("(p k) -> p k", k=NC)).then_inc(c_in, 16)
            for i in range(2):
                act.dma_start(NM[:, i, :], norm_mix[i].rearrange("(k p) -> p k", p=P)).then_inc(small_in, 16)
            act.dma_start(RW[:], router_w.rearrange("(k p) e -> p k e", p=P)).then_inc(small_in, 16)
            act.dma_start(RB[:], router_bias.partition_broadcast(P)).then_inc(small_in, 16)
            for t in range(3):
                act.dma_start(CW[:, t, :], conv_w[0, t].rearrange("(k p) -> p k", p=P)).then_inc(small_in, 16)
        act.wait_ge(c_in, 16)
        nc.scalar.activation(SC[:], CC[:], ACT.Silu).then_inc(silu_c, 1)

        norms = {"squares": 0, "roots": 0}

        def squares(src, m):
            norms["squares"] += 1
            nc.scalar.activation(SQ[:], src, ACT.Square, accum_out=SS[:, m:m + 1]).then_inc(sq_done, 1)
            act.wait_ge(sq_done, norms["squares"])

        def root(tiles=range(NT)):
            cols = slice(tiles[0], tiles[-1] + 1)
            norms["roots"] += 1
            act.wait_ge(var_ready, norms["roots"])
            nc.scalar.activation(SD[:, cols], VAR[:, cols], ACT.Sqrt).then_inc(sd_ready, 1)

        for q in range(4):
            act.wait_ge(x_in[q], 32)
            squares(XN[:, q, :], q)
            squares(XN[:, q + 4, :], q + 4)
        root()
        act.wait_ge(rs_ready, 1)
        for t in (6, 3, 7):
            nc.scalar.activation(XN[:, t, :], XN[:, t, :], ACT.Copy, scale=RS[:, t:t + 1]).then_inc(scaled, 1)

        def pt_evac(dt):
            act.wait_ge(step1_mm, dt + 1)
            nc.scalar.activation(PT[:, dt, :, 0:256], bank(dt % 2).rearrange("p (s n) -> p s n", s=2),
                                 ACT.Copy).then_inc(pt_act, 1)
            nc.scalar.activation(PT[:, dt, :, 512:640], bank(3)[:, 0:256].rearrange("p (s n) -> p s n", s=2),
                                 ACT.Copy).then_inc(pt_act, 1)

        def pt_scale(g):
            act.wait_ge(pt_dve, 2 * g + 1)
            nc.scalar.activation(PT[:, 2 * g], PT[:, 2 * g], ACT.Copy,
                                 scale=AC[:, 1, 2 * g:2 * g + 1]).then_inc(pt_scaled, 1)

        def mix_evac(ch):
            act.wait_ge(step2_mm, ch + 1)
            if ch >= 2:
                act.wait_ge(ft_dve, ch - 1)
            b = 4 + 2 * (ch % 2)
            nc.scalar.activation(VS[:, ch % 2, :], bank(b + 1)[:, 0:N_FOLD], ACT.Copy).then_inc(vs_ready, 1)
            nc.scalar.activation(FT[:, ch, 768:1024].rearrange("p (b n) -> p b n", b=2), PS[:, b:b + 2, N_FOLD:BANK],
                                 ACT.Copy).then_inc(ft_act, 1)

        for dt in range(NC):
            pt_evac(dt)
        for g in range(GROUPS):
            act.dma_start(WF[:, 2 * g:2 * g + 2, :],
                          fourier_w_out[0, g * GROUP:(g + 1) * GROUP, :].rearrange("(j r) n -> j r n", r=2)
                          ).then_inc(wf_in[g], 16)
        act.wait_ge(cols_ready, 1)
        act.wait_ge(pt_act, 2 * NC)
        pt_scale(0)
        pt_scale(1)
        for g in range(2, GROUPS):
            mix_evac(2 * g - 4)
            mix_evac(2 * g - 3)
            pt_scale(g)
        for ch in range(4, NC):
            mix_evac(ch)
        act.wait_ge(ef_ready, GROUPS)
        for m, (first, step) in enumerate(TILES):
            act.dma_start(X[:, m, :], x_rows[ds(first, P, step=step), :]).then_inc(res_in[m], 16)

        def row_evac_act(n, row, b):
            act.wait_ge(rows_mm, n)
            nc.scalar.activation(row, bank(b, 2), ACT.Copy).then_inc(row_evac, 1)

        row_evac_act(1, G1, 6)

        def tile_high(m):
            if m >= 2:
                act.wait_ge(y_mm, NT + m - 1)
            nc.scalar.activation(ZH[m % 2][:], tile_of(ZT, m), ACT.Copy).then_inc(z_high, 1)

        for layer in range(2):
            def square_of(m):
                act.wait_ge(x_ready, layer * NT + m + 1)
                if layer == 1 and m < NT - 2:
                    tile_high(m + 2)
                squares(X[:, m, :], m)

            def transposed(m):
                act.wait_ge(h_tr, layer * NT + m + 1)
                if m >= 2:
                    act.wait_ge(router_mm, layer * NT + m - 1)
                nc.scalar.activation(HTM[m % 2][:].rearrange("p c n -> p (c n)"), bank(4, 2),
                                     ACT.Copy).then_inc(hT_ready, 1)

            for m in range(4):
                square_of(m)
            if layer == 1:
                root(NORMS[0])
            if layer == 0:
                act.dma_start(NF0[:], norm_ffn[0].partition_broadcast(P)).then_inc(norm_row_in, 16)
                row_evac_act(2, SH2, 4)
            square_of(4)
            if layer == 0:
                act.wait_ge(row_evac, 3)
                row_evac_act(4, G2, 4)
            square_of(5)
            if layer == 0:
                root(NORMS[0])
            root(NORMS[1])
            transposed(0)
            transposed(1)
            square_of(6)
            for m in range(2, 6):
                transposed(m)
            root(NORMS[2])
            transposed(6)
            square_of(7)
            root(NORMS[3])
            transposed(7)
            for half in range(2):
                act.wait_ge(router_mm, layer * NT + 4 * half + 4)
                nc.scalar.activation(ST[:, half * BANK:(half + 1) * BANK], bank(6 + half)[0:EXPERTS, :],
                                     ACT.Sigmoid).then_inc(scores_T, 1)

            def xt_evac(s, par):
                act.wait_ge(xt_tr, s + (layer * MAX_SLOTS + 1))
                nc.scalar.activation(XT[par][:, 0:4, :].rearrange("p c n -> p (c n)"), bank(0),
                                     ACT.Copy).then_inc(xt_act, 1)

            def slot(s, par, more=True):
                b = layer * MAX_SLOTS
                act.wait_ge(gu_mm, s + (b + 1))
                act.wait_ge(he_ready, s + b)
                nc.scalar.activation(SG[:], bank(2)[:, 0:FF], ACT.Silu).then_inc(silu_g, 1)
                if more:
                    xt_evac(s + 1, 1 - par)

            xt_evac(0, 0)
            if layer == 0:
                act.wait_ge(gu_mm, 1)
                nc.scalar.activation(SG[:], bank(2)[:, 0:FF], ACT.Silu).then_inc(silu_g, 1)
                xt_evac(1, 1)
            else:
                slot(0, 0)
            with act.Fori(0, ALWAYS) as i:
                for k in range(2):
                    slot(2 * i + (1 + k), 1 - k)
            act.wait_ge(routed, layer + 1)
            used = slots_used(act)
            done = layer * MAX_SLOTS + 2
            with act.Fori(ALWAYS, PAIR_LOOPS) as i:
                with act.If(used > 2 * i):
                    for k in range(2):
                        slot(2 * i + (1 + k), 1 - k)
                with act.Else():
                    act.wait_ge(xt_act, 2 * i + done)
                    for sig in (silu_g, xt_act):
                        act.sem_inc(sig, 2)
            with act.If(used > 2 * PAIR_LOOPS):
                slot(MAX_SLOTS - 2, 1)
                slot(MAX_SLOTS - 1, 0, more=False)
            with act.Else():
                act.wait_ge(xt_act, 2 * PAIR_LOOPS + done)
                act.sem_inc(silu_g, 2)
                act.sem_inc(xt_act, 1)

            if layer == 0:
                for tiles in NORMS:
                    for m in tiles:
                        act.wait_ge(added, 2 * (m + 1))
                        squares(X[:, m, :], m)
                    root(tiles)
                for ch in range(NC):
                    act.wait_ge(conv_tr, ch + 1)
                    if ch >= 2:
                        act.wait_ge(hT_dve, ch - 1)
                    src = bank(2 * (ch % 2), 2)
                    for a, n, tok, step in ((0, 4 * P, 1, 2), (4 * P, 2 * P, 2, 4), (6 * P, P, 4, 8), (7 * P, P, 0, 8)):
                        ins = nc.scalar.activation(HTF[ch % 2][:, tok:SEQ:step], src[:, a:a + n], ACT.Identity,
                                                   scale=AC[:, 1, ch:ch + 1], bias=AC[:, 0, ch:ch + 1])
                    ins.then_inc(hT_act, 1)

                def high(n, par, loads, used):
                    if used is not None:
                        act.wait_ge(cin_mm, used)
                    act.wait_ge(win_in[par], loads * 16)
                    nc.scalar.activation(WINH[par][:], WINR[par][:], ACT.Copy).then_inc(win_high, 1)

                def c_gate(j):
                    act.wait_ge(cin_mm, 3 * j + 1)
                    act.wait_ge(u_ready, 2 * j)
                    for half in range(2):
                        nc.scalar.activation(CB[half][:], bank(3 * half), ACT.Copy).then_inc(cb_ready, 1)

                def b_gate(j, read):
                    act.wait_ge(cin_mm, 3 * j + 3)
                    if read is not None:
                        act.wait_ge(z_ready, read)
                    for half in range(2):
                        nc.scalar.activation(BB[:, half * BANK:(half + 1) * BANK], bank(3 * half + 2),
                                             ACT.Copy).then_inc(bb_ready, 1)

                high(0, 0, 1, None)
                high(1, 1, 1, None)
                act.wait_ge(cin_mm, 1)
                for half in range(2):
                    nc.scalar.activation(CB[half][:], bank(3 * half), ACT.Copy).then_inc(cb_ready, 1)
                high(2, 0, 2, 1)
                high(3, 1, 2, 2)
                b_gate(0, None)
                high(4, 0, 3, 3)
                c_gate(1)
                high(5, 1, 3, 4)
                with act.Fori(1, NC // 2) as i:
                    for k in range(2):
                        j, n = 2 * i + k, 6 * i + 3 * k
                        high(n, k, 3 * i + (k + 1), n - 1)
                        b_gate(2 * i + (k - 1), 2 * i + (k - 1))
                        high(n + 1, 1 - k, 3 * i + (k + 1) if k == 0 else 3 * i + 3, n)
                        c_gate(j)
                        high(n + 2, k, 3 * i + (k + 2), n + 1)
                b_gate(NC - 1, NC - 1)
                act.wait_ge(z_ready, NC)
                act.dma_start(NF[:], norm_ffn[1].partition_broadcast(P)).then_inc(norm_row_in, 16)
                act.wait_ge(wa_used, 2 * N_ADA)
                tile_high(0)
                tile_high(1)
                row_evac_act(5, G1, 6)
                row_evac_act(6, SH2, 4)
                act.wait_ge(row_evac, 7)
                row_evac_act(8, G2, 4)
                for q in range(4):
                    act.wait_ge(wout_in[q], 16)
                    nc.scalar.activation(WOH[:, 2 * q:2 * q + 2, :], WOR[:, 2 * q:2 * q + 2, :],
                                         ACT.Copy).then_inc(wout_high, 1)

    @block.vector
    def _(dve):
        V = nc.vector
        count = [0]

        def link(ins):
            count[0] += 1
            ins.then_inc(dve_step, 1)
            dve.wait_ge(dve_step, count[0])

        norms = {"squares": 0, "roots": 0}

        def rstd(tiles=range(NT)):
            cols = slice(tiles[0], tiles[-1] + 1)
            var, rs, rt = VAR[:, cols], RS[:, cols], RT[:, cols]
            norms["squares"] += len(tiles)
            norms["roots"] += 1
            dve.wait_ge(sq_done, norms["squares"])
            V.tensor_scalar(var, SS[:, cols], 1.0 / D, EPS, ALU.mult, ALU.add).then_inc(var_ready, 1)
            dve.wait_ge(sd_ready, norms["roots"])
            link(V.reciprocal(rs, SD[:, cols]))
            link(V.tensor_tensor(rt, rs, rs, ALU.mult))
            link(V.tensor_tensor(rt, rt, var, ALU.mult))
            link(V.tensor_scalar(rt, rt, -0.5, 1.5, ALU.mult, ALU.add))
            V.tensor_tensor(rs, rs, rt, ALU.mult).then_inc(rs_ready, 1)
            dve.wait_ge(rs_ready, norms["roots"])

        rstd()
        for t in (0, 4, 1, 5, 2):
            V.tensor_scalar(XN[:, t, :], XN[:, t, :], RS[:, t:t + 1], None, ALU.mult).then_inc(scaled, 1)
        dve.wait_ge(scaled, NT)
        V.tensor_tensor(FB[:], XN[:, 0:4, :], XN[:, 4:8, :], ALU.subtract).then_inc(folds, 1)
        link(V.tensor_tensor(FA[:], XN[:, 0:4, :], XN[:, 4:8, :], ALU.add))
        V.tensor_tensor(FAB[:], FA[:, 0:2, :], FA[:, 2:4, :], ALU.subtract).then_inc(folds, 1)
        link(V.tensor_tensor(FAA[:], FA[:, 0:2, :], FA[:, 2:4, :], ALU.add))
        dve.wait_ge(folds, 2)
        V.tensor_tensor(FAAB[:], FAA[:, 0, :], FAA[:, 1, :], ALU.subtract).then_inc(folds, 1)
        V.tensor_tensor(FAAA[:], FAA[:, 0, :], FAA[:, 1, :], ALU.add).then_inc(folds, 1)

        def ada_block(dst, par, loads, step_at):
            dve.wait_ge(wa_in[par], loads * 16)
            for k in range(NC):
                ins = V.scalar_tensor_tensor(out=dst, in0=WA_ALL[par][:, k, :], scalar=SC[:, k:k + 1], in1=dst,
                                             op0=ALU.mult, op1=ALU.add)
                if k < NC - 1:
                    ins.then_inc(dve_step, 1)
                    dve.wait_ge(dve_step, step_at + (k + 1))
            ins.then_inc(wa_used, 1)

        def ada_first(b):
            ada_block(ACC[:, b * ADA_BLOCK:(b + 1) * ADA_BLOCK], b % 2, (b - ADA_MIXER) // 2 + 1 + ADA_EARLY, count[0])
            count[0] += NC - 1

        dve.wait_ge(small_in, 16 * 7)
        dve.wait_ge(bias_in, 16)
        dve.wait_ge(silu_c, 1)

        def pt_evac(dt):
            dve.wait_ge(step1_mm, dt + 1)
            V.tensor_copy(PT[:, dt, :, 256:512].rearrange("p s (k n) -> p k s n", k=2),
                          bank(2).rearrange("p (k s n) -> p k s n", k=2, s=2)).then_inc(pt_dve, 1)

        for b in range(ADA_MIXER):
            ada_block(ACC[:, b * ADA_BLOCK:(b + 1) * ADA_BLOCK], b % 4, b // 4 + 1, count[0])
            count[0] += NC - 1
            pt_evac(b)
        ada_first(ADA_MIXER)
        ada_first(ADA_MIXER + 1)
        dve.wait_ge(cols_mm, 1)
        link(V.tensor_copy(AC[:, 0, :], bank(6)[:, 0:NC]))
        link(V.scalar_tensor_tensor(out=AC[:, 1, :], in0=bank(6)[:, NC:2 * NC], scalar=1.0, in1=NM[:, 0, :],
                                    op0=ALU.add, op1=ALU.mult))
        link(V.tensor_scalar(AC[:, 2, :], AC[:, 1, :], -1.0, None, ALU.mult))
        at_zero = float(SEQ / np.sqrt(SEQ * GROUP))
        pairs = AC[:, 0, :].rearrange("p (g r) -> p r g", r=2)
        link(V.tensor_tensor(SHS[:, 0, :], pairs[:, 0], pairs[:, 1], ALU.add))
        link(V.tensor_tensor(SHS[:, 1, :], pairs[:, 0], pairs[:, 1], ALU.subtract))
        V.tensor_scalar(SHS[:], SHS[:], at_zero, None, ALU.mult).then_inc(cols_ready, 1)
        dve.wait_ge(cols_ready, 1)

        def ef(g):
            dve.wait_ge(pt_scaled, g + 1)
            if g >= 2:
                dve.wait_ge(step2_mm, 2 * g - 2)
            a, b = PT[:, 2 * g], PT[:, 2 * g + 1]
            for i in range(2):
                ins = V.scalar_tensor_tensor(out=EF[g % 2][:, i], in0=b, scalar=AC[:, 1 + i, 2 * g + 1:2 * g + 2],
                                             in1=a, op0=ALU.mult, op1=ALU.add)
            link(ins)
            zero = EF[g % 2][:, :, 0, 512:513].rearrange("p i n -> p (i n)")
            V.tensor_tensor(zero, zero, SHS[:, :, g], ALU.add).then_inc(ef_ready, 1)

        def mix_evac(ch):
            dve.wait_ge(vs_ready, ch + 1)
            dve.wait_ge(ft_act, ch + 1)
            u, v = bank(4 + 2 * (ch % 2)), VS[:, ch % 2, :]
            V.tensor_tensor(FT[:, ch, 0:256], u[:, 0:256], v[:, 0:256], ALU.subtract)
            V.tensor_tensor(FT[:, ch, 512:640], u[:, 256:384], v[:, 256:384], ALU.subtract)
            V.tensor_tensor(FT[:, ch, 511:255:-1], u[:, 0:256], v[:, 0:256], ALU.add)
            V.tensor_tensor(FT[:, ch, 767:639:-1], u[:, 256:384], v[:, 256:384], ALU.add).then_inc(ft_dve, 1)

        ef(0)
        ef(1)
        for g in range(2, GROUPS):
            mix_evac(2 * g - 4)
            mix_evac(2 * g - 3)
            ef(g)
        for ch in range(4, NC):
            mix_evac(ch)
        for b in range(2, 8):
            ada_first(ADA_MIXER + b)

        def residual(n, m, b):
            dve.wait_ge(y_mm, n + 1)
            if n >= 2:
                dve.wait_ge(x_ready, n - 1)
            link(V.tensor_tensor(XS[m % 2][:], bank(b, 2), G1, ALU.mult))
            V.tensor_tensor(X[:, m, :], X[:, m, :], XS[m % 2][:], ALU.add).then_inc(x_ready, 1)

        def scale_row(layer, n, b):
            dve.wait_ge(norm_row_in, 16 * (layer + 1))
            dve.wait_ge(rows_mm, n)
            V.scalar_tensor_tensor(out=GS2, in0=bank(b, 2), scalar=1.0, in1=(NF if layer else NF0)[:], op0=ALU.add,
                                   op1=ALU.mult).then_inc(row_evac, 1)

        def tile_low(m):
            dve.wait_ge(z_high, m + 1)
            V.tensor_tensor(ZL[m % 2][:], tile_of(ZT, m), ZH[m % 2][:].bitcast(f32), ALU.subtract).then_inc(z_low, 1)

        for layer in range(2):
            n0 = layer * NT

            def branch_added(m):
                if layer == 0:
                    if m == 0:
                        dve.wait_ge(row_evac, 1)
                    dve.wait_ge(res_in[m], 16)
                residual(n0 + m, m, 2 * (m % 2))
                if layer == 1 and m < NT - 2:
                    tile_low(m + 2)
                if layer == 0 and m < 4:
                    for b in range(2):
                        ada_first(ADA_MIXER + 8 + 2 * m + b)

            def hidden(m):
                if m >= 4:
                    dve.wait_ge(h_stored[m % 4], 16 * (2 * layer + 1))
                    dve.wait_ge(h_tr, n0 + m - 3)
                link(V.scalar_tensor_tensor(out=H[m % 4][:], in0=X[:, m, :], scalar=RS[:, m:m + 1], in1=GS2,
                                            op0=ALU.mult, op1=ALU.mult))
                V.tensor_tensor(H[m % 4][:], H[m % 4][:], SH2, ALU.add).then_inc(h_ready, 1)

            for m in range(4):
                branch_added(m)
            if layer == 1:
                rstd(NORMS[0])
                dve.wait_ge(row_evac, 7)
                dve.wait_ge(rows_mm, 8)
                hidden(0)
                branch_added(4)
                hidden(1)
                hidden(2)
                branch_added(5)
                hidden(3)
            else:
                branch_added(4)
                dve.wait_ge(row_evac, 2)
                scale_row(0, 3, 6)
                branch_added(5)
                rstd(NORMS[0])
                dve.wait_ge(row_evac, 3)
                dve.wait_ge(rows_mm, 4)
                for m in range(4):
                    hidden(m)
            branch_added(6)
            rstd(NORMS[1])
            hidden(4)
            hidden(5)
            rstd(NORMS[2])
            hidden(6)
            branch_added(7)
            rstd(NORMS[3])
            hidden(7)

            def t3(i):
                return SMALL[:, i]

            def g4(a):
                return a.rearrange("p m (g e) -> p (m g) e", g=EGROUPS)

            def tiny(i, n):
                return TINY[:, i, 0:n]

            def over_e(a, n):
                return a[:, :, None].to_broadcast([P, n, PER_GROUP])

            prio = K[:, C_PRIO:C_PRIO + PER_GROUP]
            MG = NT * EGROUPS
            dve.wait_ge(scores_tr, layer + 1)
            scores, biased, eq, rank, rest = t3(0), t3(1), t3(2), t3(3), t3(4)
            first, second, m1, m2 = t3(5), t3(6), t3(7), t3(8)
            link(V.tensor_copy(scores.rearrange("p m e -> p (m e)"), bank(4)[:, 0:P]))
            link(V.tensor_tensor(biased, scores, RB[:, None, :].to_broadcast([P, NT, EXPERTS]), ALU.add))

            def first_of(dst, src, best, n, prio_b, shape):
                link(V.tensor_tensor(eq_of(n), src, best, ALU.is_equal))
                link(V.tensor_tensor(rank_of(n), eq_of(n), prio_b, ALU.mult))
                link(V.tensor_reduce(tiny(3, n), rank_of(n), X_AXIS, ALU.max))
                link(V.tensor_tensor(dst, rank_of(n), tiny(3, n)[:, :, None].to_broadcast(shape), ALU.is_equal))

            def eq_of(n):
                return g4(eq) if n == MG else tiny(4, MG).rearrange("p (m g) -> p m g", g=EGROUPS)

            def rank_of(n):
                return g4(rank) if n == MG else tiny(5, MG).rearrange("p (m g) -> p m g", g=EGROUPS)

            prio_in = prio[:, None, :].to_broadcast([P, MG, PER_GROUP])
            prio_groups = prio[:, None, :].to_broadcast([P, NT, EGROUPS])
            link(V.tensor_reduce(tiny(0, MG), g4(biased), X_AXIS, ALU.max))
            first_of(g4(first), g4(biased), over_e(tiny(0, MG), MG), MG, prio_in, [P, MG, PER_GROUP])
            link(V.scalar_tensor_tensor(out=rest, in0=first, scalar=-1e30, in1=biased, op0=ALU.mult, op1=ALU.add))
            link(V.tensor_reduce(tiny(1, MG), g4(rest), X_AXIS, ALU.max))
            first_of(g4(second), g4(rest), over_e(tiny(1, MG), MG), MG, prio_in, [P, MG, PER_GROUP])
            link(V.tensor_tensor(tiny(2, MG), tiny(0, MG), tiny(1, MG), ALU.add))
            sums = tiny(2, MG).rearrange("p (m g) -> p m g", g=EGROUPS)
            link(V.tensor_reduce(tiny(6, NT), sums, X_AXIS, ALU.max))
            in_group = tiny(7, MG)
            first_of(in_group.rearrange("p (m g) -> p m g", g=EGROUPS), sums,
                     tiny(6, NT)[:, :, None].to_broadcast([P, NT, EGROUPS]), NT, prio_groups, [P, NT, EGROUPS])
            link(V.tensor_tensor(g4(m1), g4(first), over_e(in_group, MG), ALU.mult))
            link(V.tensor_tensor(g4(m2), g4(second), over_e(in_group, MG), ALU.mult))
            both = t3(9)
            V.tensor_tensor(both, m1, m2, ALU.add).then_inc(mask_ready, 1)
            for i, mk in enumerate((m1, m2)):
                link(V.tensor_tensor(t3(10 + i), mk, scores, ALU.mult))
                link(V.tensor_reduce(tiny(8 + i, NT), t3(10 + i), X_AXIS, ALU.add))
            link(V.tensor_tensor(tiny(10, NT), tiny(8, NT), tiny(9, NT), ALU.add))
            link(V.reciprocal(tiny(11, NT), tiny(10, NT)))
            for i in range(TOP):
                link(V.tensor_tensor(tiny(8 + i, NT), tiny(8 + i, NT), tiny(11, NT), ALU.mult))
            dve.wait_ge(rank_mm, layer + 1)
            posn, total, before = t3(12), t3(13), t3(14)
            link(V.tensor_copy(posn.rearrange("p m e -> p (m e)"), bank(0)[:, 0:P]))
            link(V.tensor_copy(total.rearrange("p m e -> p (m e)"), bank(0)[:, P:2 * P]))
            link(V.memset(before[:, 0, :], 0.0))
            for m in range(1, NT):
                link(V.tensor_tensor(before[:, m, :], before[:, m - 1, :], total[:, m - 1, :], ALU.add))
            counts = tiny(12, EXPERTS)
            link(V.tensor_tensor(counts, before[:, NT - 1, :], total[:, NT - 1, :], ALU.add))
            over = t3(15).rearrange("p m e -> p (m e)").rearrange("p (e j) -> p e j", j=NT)
            link(V.tensor_tensor(over, counts[:, :, None].to_broadcast([P, EXPERTS, NT]),
                                 K[:, None, C_STEP:C_STEP + NT].to_broadcast([P, EXPERTS, NT]), ALU.is_gt))
            n_slots, start, end = tiny(13, EXPERTS), tiny(14, EXPERTS), tiny(15, EXPERTS)
            link(V.tensor_reduce(n_slots, over, X_AXIS, ALU.add))
            lower_e = SMALL[:, 16:18].rearrange("p a m e -> p (a m e)").rearrange("p (e k) -> p e k", k=EXPERTS)
            link(V.tensor_tensor(lower_e, n_slots[:, None, :].to_broadcast([P, EXPERTS, EXPERTS]),
                                 K[:, C_TRI:C_TRI + EXPERTS ** 2].rearrange("p (e k) -> p e k", k=EXPERTS), ALU.mult))
            link(V.tensor_reduce(start, lower_e, X_AXIS, ALU.add))
            link(V.tensor_tensor(end, start, n_slots, ALU.add))
            ended = SMALL[:, 18:23].rearrange("p a m e -> p (a m e)")[:, 0:MAX_SLOTS * EXPERTS].rearrange(
                "p (s e) -> p s e", e=EXPERTS)
            link(V.tensor_tensor(ended, end[:, None, :].to_broadcast([P, MAX_SLOTS, EXPERTS]),
                                 K[:, C_SLOT:C_SLOT + MAX_SLOTS][:, :, None].to_broadcast([P, MAX_SLOTS, EXPERTS]),
                                 ALU.is_le))
            link(V.tensor_reduce(tiny(16, MAX_SLOTS), ended, X_AXIS, ALU.add))
            link(V.tensor_scalar(SEID[:, 0:MAX_SLOTS], tiny(16, MAX_SLOTS), float(EXPERTS - 1), None, ALU.min))
            link(V.tensor_copy(SEID[:, MAX_SLOTS:MAX_SLOTS + 1], end[:, EXPERTS - 1:EXPERTS]))
            link(V.tensor_tensor(posn, posn, before, ALU.add))
            link(V.tensor_scalar(start, start, float(P), None, ALU.mult))
            link(V.tensor_tensor(posn, posn, start[:, None, :].to_broadcast([P, NT, EXPERTS]), ALU.add))
            for i, mk in enumerate((m1, m2)):
                link(V.tensor_tensor(t3(10 + i), mk, posn, ALU.mult))
                link(V.tensor_reduce(TINY[:, 17, i * NT:(i + 1) * NT], t3(10 + i), X_AXIS, ALU.add))
            pos = tiny(17, TOP * NT)
            POS = POSI[:].rearrange("p r m -> p (r m)")
            SLOTI, ROWI = TINY[:, 18, 0:TOP * NT].bitcast(u32), TINY[:, 19, 0:TOP * NT].bitcast(u32)
            link(V.tensor_copy(POS, pos))
            link(V.tensor_scalar(SLOTI, POS, 7, None, ALU.logical_shift_right))
            link(V.tensor_scalar(ROWI, POS, P - 1, None, ALU.bitwise_and))
            slot_f, row_f = tiny(20, TOP * NT), tiny(21, TOP * NT)
            link(V.tensor_copy(slot_f, SLOTI))
            link(V.tensor_copy(row_f, ROWI))
            A = TOP * NT
            V.tensor_tensor(ROWHOT[:], row_f[:, :, None].to_broadcast([P, A, P]),
                            K[:, None, C_ROW:C_ROW + P].to_broadcast([P, A, P]), ALU.is_equal).then_inc(hot_ready, 1)
            link(V.tensor_tensor(SLOTHOT[:, :, 1, :], slot_f[:, :, None].to_broadcast([P, A, MAX_SLOTS]),
                                 K[:, None, C_SLOT:C_SLOT + MAX_SLOTS].to_broadcast([P, A, MAX_SLOTS]), ALU.is_equal))
            for i in range(TOP):
                V.tensor_tensor(SLOTHOT[:, i * NT:(i + 1) * NT, 0, :], SLOTHOT[:, i * NT:(i + 1) * NT, 1, :],
                                K[:, C_TOKEN:C_TOKEN + NT][:, :, None].to_broadcast([P, NT, MAX_SLOTS]),
                                ALU.mult).then_inc(hot_ready, 1)
            dve.wait_ge(hot_ready, 5 * layer + 3)
            for i in range(TOP):
                V.tensor_tensor(SLOTHOT[:, i * NT:(i + 1) * NT, 1, :], SLOTHOT[:, i * NT:(i + 1) * NT, 1, :],
                                tiny(8 + i, NT)[:, :, None].to_broadcast([P, NT, MAX_SLOTS]),
                                ALU.mult).then_inc(hot_ready, 1)
            dve.wait_ge(table_mm, layer + 1)
            link(V.tensor_copy(TOKI[:], bank(5)[:, 0:MAX_SLOTS]))
            V.tensor_copy(WOF[:], bank(5)[:, MAX_SLOTS:2 * MAX_SLOTS]).then_inc(routed, 1)

            b = layer * MAX_SLOTS

            def heT_evac(s, par):
                dve.wait_ge(he_tr, s + (b + 1))
                V.tensor_copy(HET[par][:].rearrange("p f n -> p (f n)"), bank(3)[:, 0:FF]).then_inc(heT_ready, 1)

            def gated(s, par):
                dve.wait_ge(silu_g, s + (b + 1))
                V.tensor_tensor(HE[par][:], SG[:], bank(2)[:, FF:2 * FF], ALU.mult).then_inc(he_ready, 1)

            def xt_evac(s, par):
                dve.wait_ge(xt_tr, s + (b + 1))
                V.tensor_copy(XT[par][:, 4:8, :].rearrange("p c n -> p (c n)"), bank(1)).then_inc(xt_dve, 1)

            def y_evac(s, par, stored, never_stored=False):
                dve.wait_ge(yd_mm, s + (b + 1))
                if not never_stored:
                    dve.wait_ge(y_stored[par], stored * 16 + layer * SLOTS_OF[par] * 16)
                V.scalar_tensor_tensor(out=YO[par][:], in0=bank(4, 2), scalar=WOF[:, ds(s, 1)], in1=G2,
                                       op0=ALU.mult, op1=ALU.mult).then_inc(yo_ready, 1)

            def pair_slot(i, k):
                s, par = 2 * i + (1 + k), 1 - k
                heT_evac(s - 1, 1 - par)
                gated(s, par)
                xt_evac(s + 1, 1 - par)
                y_evac(s - 1, 1 - par, i)

            xt_evac(0, 0)
            gated(0, 0)
            xt_evac(1, 1)
            for s in (1, 2):
                heT_evac(s - 1, 1 - s % 2)
                gated(s, s % 2)
                xt_evac(s + 1, 1 - s % 2)
                y_evac(s - 1, 1 - s % 2, 0, never_stored=layer == 0)
            used = slots_used(dve)
            if layer == 0:
                dve.wait_ge(bias_in, 32)

            def ada_of(i, k):
                if layer == 0:
                    ada_block(ACC[:, ds((2 * i + (k - 2)) * ADA_BLOCK, ADA_BLOCK)], k, i + ADA_LOADS,
                              (2 * i + (k - 2)) * (NC - 1) + count[0])

            def pair_if_used(i):
                with dve.If(used > 2 * i):
                    for k in range(2):
                        pair_slot(i, k)
                with dve.Else():
                    dve.wait_ge(yo_ready, 2 * i + b)
                    for sig in (heT_ready, he_ready, xt_dve, yo_ready):
                        dve.sem_inc(sig, 2)

            if layer == 0:
                with dve.Fori(1, ADA_MIXER // 2 + 1) as i:
                    for k in range(2):
                        ada_of(i, k)
                        pair_slot(i, k)
                count[0] += ADA_MIXER * (NC - 1)
            with dve.Fori(1 if layer else ADA_MIXER // 2 + 1, ALWAYS) as i:
                for k in range(2):
                    pair_slot(i, k)
            with dve.Fori(ALWAYS, PAIR_LOOPS) as i:
                pair_if_used(i)
            with dve.If(used > 2 * PAIR_LOOPS):
                for s in (MAX_SLOTS - 2, MAX_SLOTS - 1, MAX_SLOTS):
                    par = s % 2
                    heT_evac(s - 1, 1 - par)
                    if s < MAX_SLOTS:
                        gated(s, par)
                    if s + 1 < MAX_SLOTS:
                        xt_evac(s + 1, 1 - par)
                    y_evac(s - 1, 1 - par, (s - 1) // 2)
            with dve.Else():
                dve.wait_ge(yo_ready, 2 * PAIR_LOOPS + b)
                dve.sem_inc(heT_ready, 3)
                dve.sem_inc(he_ready, 2)
                dve.sem_inc(xt_dve, 1)
                dve.sem_inc(yo_ready, 3)

            if layer == 0:
                dve.wait_ge(cols_mm, 2)
                link(V.tensor_copy(AC[:, 0, :], bank(6)[:, 0:NC]))
                V.scalar_tensor_tensor(out=AC[:, 1, :], in0=bank(6)[:, NC:2 * NC], scalar=1.0, in1=NM[:, 1, :],
                                       op0=ALU.add, op1=ALU.mult).then_inc(cols_ready, 1)
                dve.wait_ge(cols_ready, 2)

            for tiles in NORMS:
                for q in range(2 * tiles[0], 2 * tiles[-1] + 2):
                    n = layer * TOP * NT + q
                    dve.wait_ge(cg_in[q % 8], 16 * (2 * layer + q // 8 + 1))
                    if q % 2:
                        dve.wait_ge(added, n)
                    V.tensor_tensor(X[:, q // 2, :], X[:, q // 2, :], CG[q % 8][:], ALU.add).then_inc(added, 1)
                if layer == 0:
                    rstd(tiles)
                    for m in tiles:
                        V.tensor_scalar(XN2[:, m, :], X[:, m, :], RS[:, m:m + 1], None, ALU.mult).then_inc(xn2_ready, 1)

            if layer == 0:
                for ch in range(NC):
                    dve.wait_ge(hT_act, ch + 1)
                    V.tensor_copy(HTH[:, ch, :], HTF[ch % 2][:]).then_inc(hT_high, 1)
                    dve.wait_ge(hT_high, ch + 1)
                    V.tensor_tensor(HTL[:, ch, :], HTF[ch % 2][:], HTH[:, ch, :].bitcast(f32),
                                    ALU.subtract).then_inc(hT_dve, 1)
                V.memset(U[:, 0:1], 0.0).then_inc(u_zero, 1)
                V.memset(U[:, SEQ + 1:SEQ + 2], 0.0).then_inc(u_zero, 1)
                dve.wait_ge(u_zero, 2)
                b1 = count[0]
                per_block = 3 + 2 * (NC - 1)

                def low(n, par):
                    dve.wait_ge(win_high, n + 1)
                    V.tensor_tensor(WINL[par][:], WINR[par][:], WINH[par][:].bitcast(f32),
                                    ALU.subtract).then_inc(win_low, 1)

                def taps(j):
                    dve.wait_ge(cin_mm, 3 * j + 2)
                    for half in range(2):
                        dve.wait_ge(cb_ready, 2 * j + (half + 1))
                        V.tensor_tensor(U[:, 1 + half * BANK:1 + (half + 1) * BANK], CB[half][:],
                                        bank(3 * half + 1), ALU.mult).then_inc(u_ready, 1)
                    dve.wait_ge(u_ready, 2 * j + 2)
                    at = j * per_block + b1
                    V.tensor_scalar(Z[:], U[:, 1:SEQ + 1], CW[:, 1, ds(j, 1)], None, ALU.mult).then_inc(dve_step, 1)
                    dve.wait_ge(dve_step, at + 1)
                    V.scalar_tensor_tensor(out=Z[:], in0=U[:, 0:SEQ], scalar=CW[:, 0, ds(j, 1)], in1=Z[:],
                                           op0=ALU.mult, op1=ALU.add).then_inc(dve_step, 1)
                    dve.wait_ge(dve_step, at + 2)
                    V.scalar_tensor_tensor(out=Z[:], in0=U[:, 2:SEQ + 2], scalar=CW[:, 2, ds(j, 1)], in1=Z[:],
                                           op0=ALU.mult, op1=ALU.add).then_inc(dve_step, 1)

                def gate(j):
                    at = j * per_block + (3 + b1)
                    dve.wait_ge(dve_step, at)
                    dve.wait_ge(bb_ready, 2 * j + 2)
                    V.tensor_tensor(ZT[:, ds(j, 1), :].rearrange("p a n -> p (a n)"), Z[:], BB[:],
                                    ALU.mult).then_inc(z_ready, 1)
                    dve.wait_ge(z_ready, j + 1)
                    for k in range(2):
                        ada_block(ACC[:, ds((2 * j + (ADA_MIXER + k)) * ADA_BLOCK, ADA_BLOCK)], k,
                                  j + (ADA_LOADS + ADA_MIXER // 2 + 1), j * per_block + (3 + k * (NC - 1) + b1))

                for j in range(2):
                    low(3 * j, j)
                    if j:
                        gate(0)
                    low(3 * j + 1, 1 - j)
                    low(3 * j + 2, j)
                    taps(j)
                with dve.Fori(1, NC // 2) as i:
                    for k in range(2):
                        low(6 * i + 3 * k, k)
                        gate(2 * i + (k - 1))
                        low(6 * i + (3 * k + 1), 1 - k)
                        low(6 * i + (3 * k + 2), k)
                        taps(2 * i + k)
                gate(NC - 1)
                count[0] += per_block * NC
                tile_low(0)
                dve.wait_ge(row_evac, 6)
                scale_row(1, 7, 6)
                tile_low(1)
                for q in range(4):
                    dve.wait_ge(wout_high, q + 1)
                    V.tensor_tensor(WOL[:, 2 * q:2 * q + 2, :], WOR[:, 2 * q:2 * q + 2, :],
                                    WOH[:, 2 * q:2 * q + 2, :].bitcast(f32), ALU.subtract).then_inc(wout_low, 1)

    @block.tensor
    def _(pe):
        T = nc.tensor

        def columns():
            for j in range(2 * NC):
                ins = T.matmul(bank(6)[:, j:j + 1], ACC[:, j * P:(j + 1) * P], ones[:, 0:1], start=True, stop=True)
            ins.then_inc(cols_mm, 1)

        def row(piece, b):
            for h in range(2):
                ins = T.matmul(bank(b + h), ones, ACC[:, piece * D + h * BANK:piece * D + (h + 1) * BANK],
                               start=True, stop=True)
            ins.then_inc(rows_mm, 1)

        def step1(dt):
            if dt >= 2:
                pe.wait_ge(pt_act, 2 * dt - 3)
            cs = slice(dt * P, (dt + 1) * P)
            pe.wait_ge(folds, 1)
            for t in range(4):
                T.matmul(bank(dt % 2), FB[:, t, cs], TB[:, t * 512:(t + 1) * 512], start=t == 0, stop=t == 3)
            if dt >= 1:
                pe.wait_ge(pt_dve, dt)
            pe.wait_ge(folds, 2)
            for t in range(2):
                T.matmul(bank(2)[:, 0:256], FAB[:, t, cs], TB[:, 2048 + t * 256:2304 + t * 256],
                         start=t == 0, stop=t == 1)
            pe.wait_ge(folds, 4)
            T.matmul(bank(2)[:, 256:512], FAAB[:, cs], TB[:, 2560:2816], start=True, stop=True)
            if dt >= 1:
                pe.wait_ge(pt_act, 2 * dt)
            T.matmul(bank(3)[:, 0:256], FAAA[:, cs], TB[:, 2816:3072], start=True, stop=True).then_inc(step1_mm, 1)

        def step2(g):
            pe.wait_ge(ef_ready, g + 1)
            for r in range(2):
                ch = 2 * g + r
                cos, sin, msin = (TB[:, 3072 + (3 * r + i) * P:3072 + (3 * r + i + 1) * P] for i in range(3))
                e = EF[g % 2][:, r]
                b = 4 + 2 * (ch % 2)
                if ch >= 2:
                    pe.wait_ge(ft_act, ch - 1)
                    pe.wait_ge(ft_dve, ch - 1)
                T.matmul(bank(b)[:, 0:N_FOLD], cos, e[:, 0, 0:N_FOLD], start=True, stop=True)
                for i in range(2):
                    at = N_FOLD + i * P
                    T.matmul(bank(b + i)[:, N_FOLD:BANK], cos, e[:, 0, at:at + P], start=True, stop=False)
                    T.matmul(bank(b + i)[:, N_FOLD:BANK], msin, e[:, 1, at:at + P], start=False, stop=True)
                T.matmul(bank(b + 1)[:, 0:N_FOLD], sin, e[:, 1, 0:N_FOLD], start=True, stop=True).then_inc(step2_mm, 1)

        pe.wait_ge(consts_in, 16)
        pe.wait_ge(tables_in, 16)
        for dt in range(NC):
            step1(dt)
        pe.wait_ge(wa_used, ADA_MIXER)
        columns()
        for g in range(GROUPS):
            step2(g)
        pe.wait_ge(ft_dve, NC)
        pe.wait_ge(ft_act, NC)
        def fourier_out(m):
            b = 2 * (m % 2)
            if m >= 2:
                pe.wait_ge(x_ready, m - 1)
            for ch in range(NC):
                if m == 0 and ch % 2 == 0:
                    pe.wait_ge(wf_in[ch // 2], 16)
                for h in range(2):
                    ins = T.matmul(bank(b + h), FT[:, ch, m * P:(m + 1) * P], WF[:, ch, h * BANK:(h + 1) * BANK],
                                   start=ch == 0, stop=ch == NC - 1)
            ins.then_inc(y_mm, 1)
            if m == 0:
                pe.wait_ge(wa_used, ADA_MIXER + D // ADA_BLOCK)
                row(2, 6)
            if m == 4:
                pe.wait_ge(wa_used, N_ADA)
                row(3, 4)
                pe.wait_ge(row_evac, 1)
                row(4, 6)
            if m == 5:
                pe.wait_ge(row_evac, 2)
                row(5, 4)

        def conv_out(m):
            b = 2 * (m % 2)
            if m >= 2:
                pe.wait_ge(x_ready, NT + m - 1)
            pe.wait_ge(z_low, m + 1)
            for ch in range(NC):
                if m == 0 and ch % 2 == 0:
                    pe.wait_ge(wout_low, ch // 2 + 1)
                for i, (z, w) in enumerate(((ZH, WOH), (ZH, WOL), (ZL, WOH))):
                    for h in range(2):
                        ins = T.matmul(bank(b + h), z[m % 2][:, ch, :], w[:, ch, h * BANK:(h + 1) * BANK],
                                       start=ch == 0 and i == 0, stop=ch == NC - 1 and i == 2)
            ins.then_inc(y_mm, 1)

        for layer in range(2):
            n0, b0 = layer * NT, layer * MAX_SLOTS
            mixer_out = conv_out if layer else fourier_out

            def router(m):
                pe.wait_ge(hT_ready, n0 + m + 1)
                for ch in range(NC):
                    ins = T.matmul(bank(6, 2)[0:EXPERTS, m * P:(m + 1) * P], RW[:, ch, :], HTM[m % 2][:, ch, :],
                                   start=ch == 0, stop=ch == NC - 1)
                ins.then_inc(router_mm, 1)

            def hidden_transposed(m):
                if m == 0:
                    pe.wait_ge(row_evac, 4 * (layer + 1))
                else:
                    pe.wait_ge(hT_ready, n0 + m)
                pe.wait_ge(h_ready, n0 + m + 1)
                for ch in range(NC):
                    ins = T.transpose(bank(4, 2)[:, ch * P:(ch + 1) * P], H[m % 4][:, ch * P:(ch + 1) * P], ident)
                ins.then_inc(h_tr, 1)

            for m in range(NT - 1):
                mixer_out(m)
            hidden_transposed(0)
            for m in range(5):
                hidden_transposed(m + 1)
                router(m)
            mixer_out(NT - 1)
            router(5)
            hidden_transposed(6)
            router(6)
            hidden_transposed(7)
            router(7)
            for half in range(2):
                pe.wait_ge(scores_T, 2 * layer + half + 1)
                for m in range(4 * half, 4 * half + 4):
                    ins = T.transpose(bank(4)[:, m * EXPERTS:(m + 1) * EXPERTS], ST[:, m * P:(m + 1) * P],
                                      ident[0:EXPERTS, 0:EXPERTS])
            ins.then_inc(scores_tr, 1)
            both = SMALL[:, 9].rearrange("p m e -> p (m e)")
            pe.wait_ge(mask_ready, layer + 1)
            T.matmul(bank(0)[:, 0:P], lower, both, start=True, stop=True)
            T.matmul(bank(0)[:, P:2 * P], ones, both, start=True, stop=True).then_inc(rank_mm, 1)
            pe.wait_ge(hot_ready, 5 * (layer + 1))
            for a in range(TOP * NT):
                ins = T.matmul(bank(5)[:, 0:2 * MAX_SLOTS], ROWHOT[:, a, :], SLOTHOT[:, a].rearrange("p k s -> p (k s)"),
                               start=a == 0, stop=a == TOP * NT - 1)
            ins.then_inc(table_mm, 1)

            def transposes(s, par, nth):
                pe.wait_ge(gathered[layer][par], nth * 16)
                for ch in range(NC):
                    ins = T.transpose(bank(0, 2)[:, ch * P:(ch + 1) * P], XG[par][:, ch * P:(ch + 1) * P], ident)
                ins.then_inc(xt_tr, 1)

            def gate_up(s, par, nth):
                pe.wait_ge(xt_act, s + (b0 + 1))
                pe.wait_ge(xt_dve, s + (b0 + 1))
                pe.wait_ge(wgu_in[par], nth * 32 + layer * SLOTS_OF[par] * 32)
                for ch in range(NC):
                    ins = T.matmul(bank(2), XT[par][:, ch, :], WGU[par][:, ch, :], start=ch == 0, stop=ch == NC - 1)
                ins.then_inc(gu_mm, 1)

            def hidden_transposes(s, par):
                for f in range(FF // P):
                    ins = T.transpose(bank(3)[:, f * P:(f + 1) * P], HE[par][:, f * P:(f + 1) * P], ident)
                ins.then_inc(he_tr, 1)

            def down(s, par, nth):
                pe.wait_ge(heT_ready, s + (b0 + 1))
                pe.wait_ge(wd_in[par], nth * 16 + layer * SLOTS_OF[par] * 16)
                for h in range(2):
                    for f in range(FF // P):
                        ins = T.matmul(bank(4 + h), HET[par][:, f, :], WD[par][:, f, h * BANK:(h + 1) * BANK],
                                       start=f == 0, stop=f == FF // P - 1)
                ins.then_inc(yd_mm, 1)

            def slot(s, par, nth, prev_nth, next_nth, more=True, last=False):
                pe.wait_ge(he_ready, s + b0)
                if not last:
                    gate_up(s, par, nth)
                hidden_transposes(s - 1, 1 - par)
                if more:
                    transposes(s + 1, 1 - par, next_nth)
                pe.wait_ge(yo_ready, s + (b0 - 1))
                down(s - 1, 1 - par, prev_nth)

            pe.wait_ge(routed, layer + 1)
            transposes(0, 0, 1)
            gate_up(0, 0, 1)
            transposes(1, 1, 1)
            pe.wait_ge(he_ready, 1 + b0)
            gate_up(1, 1, 1)
            hidden_transposes(0, 0)
            transposes(2, 0, 2)
            down(0, 0, 1)
            slot(2, 0, 2, 1, 2)
            with pe.Fori(1, ALWAYS) as i:
                slot(2 * i + 1, 1, i + 1, i + 1, i + 2)
                slot(2 * i + 2, 0, i + 2, i + 1, i + 2)
            used = slots_used(pe)
            with pe.Fori(ALWAYS, PAIR_LOOPS) as i:
                with pe.If(used > 2 * i):
                    slot(2 * i + 1, 1, i + 1, i + 1, i + 2)
                    slot(2 * i + 2, 0, i + 2, i + 1, i + 2)
                with pe.Else():
                    pe.wait_ge(yd_mm, 2 * i + b0)
                    for sig in (xt_tr, gu_mm, he_tr, yd_mm):
                        pe.sem_inc(sig, 2)
            n = PAIR_LOOPS
            with pe.If(used > 2 * n):
                slot(MAX_SLOTS - 2, 1, n + 1, n + 1, n + 2)
                slot(MAX_SLOTS - 1, 0, n + 2, n + 1, 0, more=False)
                slot(MAX_SLOTS, 1, 0, n + 2, 0, more=False, last=True)
            with pe.Else():
                pe.wait_ge(yd_mm, 2 * n + b0)
                pe.sem_inc(xt_tr, 1)
                pe.sem_inc(gu_mm, 2)
                pe.sem_inc(he_tr, 3)
                pe.sem_inc(yd_mm, 3)

            if layer == 0:
                pe.wait_ge(wa_used, N_ADA + ADA_MIXER)
                columns()
                pe.wait_ge(xn2_ready, NT)
                for ch in range(NC):
                    if ch >= 2:
                        pe.wait_ge(hT_act, ch - 1)
                        pe.wait_ge(hT_dve, ch - 1)
                    for m in range(NT):
                        ins = T.transpose(bank(2 * (ch % 2), 2)[:, m * P:(m + 1) * P],
                                          XN2[:, m, ch * P:(ch + 1) * P], ident)
                    ins.then_inc(conv_tr, 1)
                pe.wait_ge(hT_act, NC)
                pe.wait_ge(hT_dve, NC)

                def cin(n, par, idx, read):
                    pe.wait_ge(win_low, n + 1)
                    if read is not None:
                        pe.wait_ge((cb_ready, u_ready, bb_ready)[idx], read)
                    for ch in range(NC):
                        for half in range(2):
                            b, cols = 3 * half + idx, slice(half * BANK, (half + 1) * BANK)
                            T.matmul(bank(b), WINH[par][:, ch, :], HTH[:, ch, cols], start=ch == 0, stop=False)
                            T.matmul(bank(b), WINH[par][:, ch, :], HTL[:, ch, cols], start=False, stop=False)
                        for half in range(2):
                            b, cols = 3 * half + idx, slice(half * BANK, (half + 1) * BANK)
                            ins = T.matmul(bank(b), WINL[par][:, ch, :], HTH[:, ch, cols], start=False,
                                           stop=ch == NC - 1)
                    ins.then_inc(cin_mm, 1)

                for j in range(2):
                    for idx in range(3):
                        cin(3 * j + idx, (j + idx) % 2, idx, 2 if j else None)
                with pe.Fori(1, NC // 2) as i:
                    for k in range(2):
                        for idx in range(3):
                            cin(6 * i + (3 * k + idx), (k + idx) % 2, idx, 4 * i + 2 * k)
                pe.wait_ge(wa_used, 2 * N_ADA)
                row(2, 6)
                pe.wait_ge(bb_ready, 2 * NC)
                row(3, 4)
                pe.wait_ge(row_evac, 5)
                row(4, 6)
                pe.wait_ge(row_evac, 6)
                row(5, 4)
                pe.wait_ge(z_ready, NC)

    top.close()


INPUTS = ["x", "c", "w_ada", "b_ada", "norm_mix", "norm_ffn", "fourier_w_out", "conv_w_in", "conv_w", "conv_w_out",
          "router_w", "router_bias", "moe_w_gate", "moe_w_up", "moe_w_down"]


def kernel(**inputs):
    import numpy as _np
    import concourse.bacc as _bacc
    from concourse import mybir as _mybir
    from concourse.bass_utils import run_bass_kernel_spmd as _run

    nc = _bacc.Bacc("TRN2", target_bir_lowering=False, num_devices=1)
    arrays, args = {}, []
    given = [(name, inputs[name]) for name in INPUTS] + [("tables", dft_tables()), ("constants", shape_constants())]
    for name, value in given:
        a = _np.ascontiguousarray(value)
        arrays[f"in_{name}_dram"] = a
        args.append(nc.dram_tensor(f"in_{name}_dram", a.shape, _mybir.dt.from_np(a.dtype), kind="ExternalInput").ap())
    out = nc.dram_tensor("out_0_dram", (1, SEQ, D), _mybir.dt.float32, kind="ExternalOutput").ap()
    backbone(nc, *args, out)
    r = _run(nc, [arrays], core_ids=[0])
    return r.results[0]["out_0_dram"]
```
